# Optimizing a Trainium2 kernel written in Bass

```python
import math
import jax, jax.numpy as jnp
from jax import lax
import numpy as np

D_MODEL = 2048
BATCH = 1
SEQ = 256
DEPTH = 1
DEC_BATCH = 8
DEC_SEQ = 4
PAST_LEN = 1024
PAGE_SIZE = 128

D_MIX = D_MODEL
D_SSD = D_MIX // 2
SSD_HEAD_DIM = 64
SSD_HEADS = D_SSD // SSD_HEAD_DIM
SSD_GROUPS = 2
SSD_STATE = 128
SSD_CONV = 4
SSD_CHUNK = 128
CONV_DIM = D_SSD + 2 * SSD_GROUPS * SSD_STATE
D_ATT = D_MIX - D_SSD
ATT_HEAD_DIM = 128
ATT_HEADS = D_ATT // ATT_HEAD_DIM
Q_BLOCK = 128
SB_BIAS_INIT = -7.0
D_FF = 5632
FFN_CONV = 3
IN_DIM = D_SSD + CONV_DIM + SSD_HEADS + 3 * D_ATT
EPS = 1e-6

kernel_name = 'hybrid_ssd_stickbreak_convffn_step'

def rmsnorm(x, g):
    x32 = x.astype(jnp.float32)
    y = x32 * lax.rsqrt(jnp.mean(x32 * x32, axis=-1, keepdims=True) + EPS)
    return (y * g.astype(jnp.float32)).astype(x.dtype)

def causal_dwconv(u, w, b, ctx):
    L = u.shape[1]
    K = w.shape[0]
    up = jnp.concatenate([ctx.astype(u.dtype), u], axis=1)
    y = up[:, 0:L, :] * w[0]
    for k in range(1, K):
        y = y + up[:, k:k + L, :] * w[k]
    return y + b, up[:, up.shape[1] - (K - 1):, :]

def ssd_chunked(xs, dt, a, bm, cm, h0, chunk):
    b, L, H, P = xs.shape
    G, N = bm.shape[2], bm.shape[3]
    nc = L // chunk
    f32 = jnp.float32
    xdt = (xs.astype(f32) * dt[..., None]).reshape(b, nc, chunk, H, P)
    bh = jnp.repeat(bm.astype(f32), H // G, axis=2).reshape(b, nc, chunk, H, N)
    ch = jnp.repeat(cm.astype(f32), H // G, axis=2).reshape(b, nc, chunk, H, N)
    acum = jnp.cumsum((dt * a).reshape(b, nc, chunk, H), axis=2)
    causal = jnp.tril(jnp.ones((chunk, chunk), bool))[None, None, :, :, None]
    seg = acum[:, :, :, None, :] - acum[:, :, None, :, :]
    decay = jnp.where(causal, jnp.exp(jnp.where(causal, seg, 0.0)), 0.0)
    scores = jnp.einsum('bclhn,bcshn->bclsh', ch, bh) * decay
    y_diag = jnp.einsum('bclsh,bcshp->bclhp', scores, xdt)
    decay_end = jnp.exp(acum[:, :, -1:, :] - acum)
    states = jnp.einsum('bclhn,bclh,bclhp->bchpn', bh, decay_end, xdt)
    chunk_decay = jnp.exp(acum[:, :, -1, :])

    def step(hc, inp):
        s, dcy = inp
        return dcy[:, :, None, None] * hc + s, hc

    h_final, h_prev = lax.scan(step, h0.astype(f32),
                               (jnp.moveaxis(states, 1, 0), jnp.moveaxis(chunk_decay, 1, 0)))
    h_prev = jnp.moveaxis(h_prev, 0, 1)
    y_off = jnp.einsum('bclhn,bchpn,bclh->bclhp', ch, h_prev, jnp.exp(acum))
    return (y_diag + y_off).reshape(b, L, H, P), h_final

def sb_block(q, qpos, k, v, kpos, bias):
    z = jnp.einsum('bhqd,bhkd->bhqk', q, k, preferred_element_type=jnp.float32) * (ATT_HEAD_DIM ** -0.5)
    z = z + bias.astype(jnp.float32)[None, :, None, None]
    mask = (kpos[None, :] < qpos[:, None])[None, None]
    log_1m = jnp.where(mask, jax.nn.log_sigmoid(-z), 0.0)
    tail = lax.cumsum(log_1m, axis=3, reverse=True) - log_1m
    w = jnp.where(mask, jnp.exp(jax.nn.log_sigmoid(z) + tail), 0.0)
    return jnp.einsum('bhqk,bhkd->bhqd', w.astype(v.dtype), v)

def sb_attention(q, k, v, q_pos0, bias):
    b, Lq, H, d = q.shape
    qt = q.transpose(0, 2, 1, 3)
    kt = k.transpose(0, 2, 1, 3)
    vt = v.transpose(0, 2, 1, 3)
    kpos = jnp.arange(k.shape[1])
    qpos = q_pos0 + jnp.arange(Lq)
    if Lq % Q_BLOCK == 0 and Lq > Q_BLOCK:
        nb = Lq // Q_BLOCK
        qb = qt.reshape(b, H, nb, Q_BLOCK, d).transpose(2, 0, 1, 3, 4)
        ob = lax.map(lambda a: sb_block(a[0], a[1], kt, vt, kpos, bias), (qb, qpos.reshape(nb, Q_BLOCK)))
        o = ob.transpose(1, 2, 0, 3, 4).reshape(b, H, Lq, d)
    else:
        o = sb_block(qt, qpos, kt, vt, kpos, bias)
    return o.transpose(0, 2, 1, 3).reshape(b, Lq, H * d)

def mixer(h, lw, conv_ctx, ssm_h0, k_past, v_past):
    b, L, _ = h.shape
    proj = h @ lw['w_in']
    o1 = D_SSD
    o2 = o1 + CONV_DIM
    o3 = o2 + SSD_HEADS
    o4 = o3 + D_ATT
    o5 = o4 + D_ATT
    z, xbc, dt_raw, q, k, v = jnp.split(proj, [o1, o2, o3, o4, o5], axis=-1)
    xbc, conv_new = causal_dwconv(xbc, lw['conv_w'], lw['conv_b'], conv_ctx)
    xbc = jax.nn.silu(xbc)
    xs, bm, cm = jnp.split(xbc, [D_SSD, D_SSD + SSD_GROUPS * SSD_STATE], axis=-1)
    xs = xs.reshape(b, L, SSD_HEADS, SSD_HEAD_DIM)
    dt = jax.nn.softplus(dt_raw.astype(jnp.float32) + lw['dt_bias'].astype(jnp.float32))
    a = -jnp.exp(lw['a_log'].astype(jnp.float32))
    chunk = SSD_CHUNK if L % SSD_CHUNK == 0 else L
    y, ssm_new = ssd_chunked(xs, dt, a,
                             bm.reshape(b, L, SSD_GROUPS, SSD_STATE),
                             cm.reshape(b, L, SSD_GROUPS, SSD_STATE), ssm_h0, chunk)
    y = y.astype(h.dtype) + lw['d_skip'][:, None] * xs
    y = y.reshape(b, L, D_SSD) * jax.nn.silu(z)
    y = rmsnorm(y.reshape(b, L, SSD_GROUPS, D_SSD // SSD_GROUPS),
                lw['g_ssd_norm'].reshape(SSD_GROUPS, D_SSD // SSD_GROUPS)).reshape(b, L, D_SSD)
    kh = k.reshape(b, L, ATT_HEADS, ATT_HEAD_DIM)
    vh = v.reshape(b, L, ATT_HEADS, ATT_HEAD_DIM)
    if k_past is None:
        k_all, v_all, pos0 = kh, vh, 0
    else:
        k_all = jnp.concatenate([k_past.astype(kh.dtype), kh], axis=1)
        v_all = jnp.concatenate([v_past.astype(vh.dtype), vh], axis=1)
        pos0 = k_past.shape[1]
    o = sb_attention(q.reshape(b, L, ATT_HEADS, ATT_HEAD_DIM), k_all, v_all, pos0, lw['sb_bias'])
    out = jnp.concatenate([y, o], axis=-1) @ lw['w_out']
    return out, kh, vh, ssm_new, conv_new

def conv_ffn(h, lw, ctx):
    u = h @ lw['w_ffn_in']
    uc, new_ctx = causal_dwconv(u, lw['ffn_conv_w'], lw['ffn_conv_b'], ctx)
    gate, val = jnp.split(uc, 2, axis=-1)
    return (jax.nn.silu(gate) * val) @ lw['w_ffn_out'], new_ctx

def decoder_layer(x, c, lw, conv_ctx, ssm_h0, ffn_ctx, k_past, v_past):
    mod = jax.nn.silu(c) @ lw['w_ada'] + lw['b_ada']
    sh1, sc1, g1, sh2, sc2, g2 = jnp.split(mod[:, None, :], 6, axis=-1)
    h = rmsnorm(x, lw['g_pre_mix']) * (1 + sc1) + sh1
    m, k_new, v_new, ssm_new, conv_new = mixer(h, lw, conv_ctx, ssm_h0, k_past, v_past)
    x = x + g1 * rmsnorm(m, lw['g_post_mix'])
    h = rmsnorm(x, lw['g_pre_ffn']) * (1 + sc2) + sh2
    f, ffn_new = conv_ffn(h, lw, ffn_ctx)
    x = x + g2 * rmsnorm(f, lw['g_post_ffn'])
    return x, (k_new, v_new, ssm_new, conv_new, ffn_new)

def setup_inputs(seed: int = 0) -> dict:
    key = jax.random.key(seed)
    ks = jax.random.split(key, 32)
    f32 = jnp.float32
    n_pages = PAST_LEN // PAGE_SIZE
    n_pool = (DEC_BATCH * n_pages * 5) // 4

    def nrm(k, shape, scale):
        return jax.random.normal(k, shape, f32) * scale

    def gain(k, shape):
        return 1.0 + 0.05 * jax.random.normal(k, shape, f32)

    dt0 = jnp.exp(jax.random.uniform(ks[24], (DEPTH, SSD_HEADS), f32, math.log(1e-3), math.log(1e-1)))
    return {
        'x_prompt': nrm(ks[0], (BATCH, SEQ, D_MODEL), 1.0),
        'x_sample': nrm(ks[1], (DEC_BATCH, DEC_SEQ, D_MODEL), 1.0),
        'c_prompt': nrm(ks[2], (BATCH, D_MODEL), 1.0),
        'c_sample': nrm(ks[3], (DEC_BATCH, D_MODEL), 1.0),
        'cache_k': nrm(ks[4], (DEPTH, n_pool, PAGE_SIZE, ATT_HEADS, ATT_HEAD_DIM), 1.0),
        'cache_v': nrm(ks[5], (DEPTH, n_pool, PAGE_SIZE, ATT_HEADS, ATT_HEAD_DIM), 1.0),
        'page_table': jax.random.permutation(ks[6], n_pool)[: DEC_BATCH * n_pages]
                      .reshape(DEC_BATCH, n_pages).astype(jnp.int32),
        'state_ssm': nrm(ks[7], (DEPTH, DEC_BATCH, SSD_HEADS, SSD_HEAD_DIM, SSD_STATE), 0.5),
        'state_conv': nrm(ks[8], (DEPTH, DEC_BATCH, SSD_CONV - 1, CONV_DIM), 1.0),
        'state_ffn_conv': nrm(ks[9], (DEPTH, DEC_BATCH, FFN_CONV - 1, 2 * D_FF), 1.0),
        'w_ada': nrm(ks[10], (DEPTH, D_MODEL, 6 * D_MODEL), D_MODEL ** -0.5),
        'b_ada': nrm(ks[11], (DEPTH, 6 * D_MODEL), 0.01),
        'g_pre_mix': gain(ks[12], (DEPTH, D_MODEL)),
        'g_post_mix': gain(ks[13], (DEPTH, D_MODEL)),
        'g_pre_ffn': gain(ks[14], (DEPTH, D_MODEL)),
        'g_post_ffn': gain(ks[15], (DEPTH, D_MODEL)),
        'w_in': nrm(ks[16], (DEPTH, D_MODEL, IN_DIM), D_MODEL ** -0.5),
        'conv_w': nrm(ks[17], (DEPTH, SSD_CONV, CONV_DIM), SSD_CONV ** -0.5),
        'conv_b': nrm(ks[18], (DEPTH, CONV_DIM), 0.01),
        'dt_bias': dt0 + jnp.log(-jnp.expm1(-dt0)),
        'a_log': jnp.log(jax.random.uniform(ks[19], (DEPTH, SSD_HEADS), f32, 1.0, 16.0)),
        'd_skip': gain(ks[20], (DEPTH, SSD_HEADS)),
        'g_ssd_norm': gain(ks[21], (DEPTH, D_SSD)),
        'sb_bias': SB_BIAS_INIT + 0.3 * jax.random.normal(ks[28], (DEPTH, ATT_HEADS), f32),
        'w_out': nrm(ks[22], (DEPTH, D_MIX, D_MODEL), D_MIX ** -0.5),
        'w_ffn_in': nrm(ks[23], (DEPTH, D_MODEL, 2 * D_FF), D_MODEL ** -0.5),
        'ffn_conv_w': nrm(ks[25], (DEPTH, FFN_CONV, 2 * D_FF), FFN_CONV ** -0.5),
        'ffn_conv_b': nrm(ks[26], (DEPTH, 2 * D_FF), 0.01),
        'w_ffn_out': nrm(ks[27], (DEPTH, D_FF, D_MODEL), D_FF ** -0.5),
    }

def reference(x_prompt, x_sample, c_prompt, c_sample, cache_k, cache_v, page_table,
              state_ssm, state_conv, state_ffn_conv, w_ada, b_ada, g_pre_mix, g_post_mix,
              g_pre_ffn, g_post_ffn, w_in, conv_w, conv_b, dt_bias, a_log, d_skip,
              g_ssd_norm, sb_bias, w_out, w_ffn_in, ffn_conv_w, ffn_conv_b, w_ffn_out):
    n_seq, n_pages = page_table.shape
    past = n_pages * PAGE_SIZE
    bp = x_prompt.shape[0]
    yp, ys = x_prompt, x_sample
    p_states, s_states = [], []
    for l in range(DEPTH):
        lw = dict(w_ada=w_ada[l], b_ada=b_ada[l], g_pre_mix=g_pre_mix[l], g_post_mix=g_post_mix[l],
                  g_pre_ffn=g_pre_ffn[l], g_post_ffn=g_post_ffn[l], w_in=w_in[l], conv_w=conv_w[l],
                  conv_b=conv_b[l], dt_bias=dt_bias[l], a_log=a_log[l], d_skip=d_skip[l],
                  g_ssd_norm=g_ssd_norm[l], sb_bias=sb_bias[l], w_out=w_out[l], w_ffn_in=w_ffn_in[l],
                  ffn_conv_w=ffn_conv_w[l], ffn_conv_b=ffn_conv_b[l], w_ffn_out=w_ffn_out[l])
        conv0 = jnp.zeros((bp, SSD_CONV - 1, CONV_DIM), yp.dtype)
        ssm0 = jnp.zeros((bp, SSD_HEADS, SSD_HEAD_DIM, SSD_STATE), jnp.float32)
        ffn0 = jnp.zeros((bp, FFN_CONV - 1, 2 * D_FF), yp.dtype)
        yp, sp = decoder_layer(yp, c_prompt, lw, conv0, ssm0, ffn0, None, None)
        p_states.append(sp)
        k_past = cache_k[l][page_table].reshape(n_seq, past, ATT_HEADS, ATT_HEAD_DIM)
        v_past = cache_v[l][page_table].reshape(n_seq, past, ATT_HEADS, ATT_HEAD_DIM)
        ys, ss = decoder_layer(ys, c_sample, lw, state_conv[l], state_ssm[l], state_ffn_conv[l],
                               k_past, v_past)
        s_states.append(ss)
    k_prompt = jnp.stack([s[0] for s in p_states])
    v_prompt = jnp.stack([s[1] for s in p_states])
    ssm_prompt = jnp.stack([s[2] for s in p_states])
    conv_prompt = jnp.stack([s[3] for s in p_states])
    ffn_conv_prompt = jnp.stack([s[4] for s in p_states])
    k_sample = jnp.stack([s[0] for s in s_states])
    v_sample = jnp.stack([s[1] for s in s_states])
    ssm_sample = jnp.stack([s[2] for s in s_states])
    conv_sample = jnp.stack([s[3] for s in s_states])
    ffn_conv_sample = jnp.stack([s[4] for s in s_states])
    return (yp, ys, k_prompt, v_prompt, ssm_prompt, conv_prompt, ffn_conv_prompt,
            k_sample, v_sample, ssm_sample, conv_sample, ffn_conv_sample)


_drawn_inputs = setup_inputs


def setup_inputs(seed=0):
    import zlib

    import numpy as np

    out = dict(_drawn_inputs(seed))
    spreads = {}
    factors = {'conv_b': 3.86,
     'd_skip': 51.502,
     'sb_bias': 29.488,
     'ffn_conv_b': 8.0,
     'cache_k': 8.0,
     'cache_v': 8.0}
    for name, (base, spread) in spreads.items():
        noise = np.random.default_rng([zlib.crc32(name.encode()), seed]).standard_normal(out[name].shape)
        drawn = base * np.exp(spread * noise) if base else spread * noise
        out[name] = __import__('jax').numpy.asarray(drawn.astype(out[name].dtype))
    for name, factor in factors.items():
        out[name] = (out[name] * factor).astype(out[name].dtype)
    return out
```

```python
from contextlib import ExitStack

import concourse.bass as bass
from concourse import mybir

F32 = mybir.dt.float32
F32R = mybir.dt.float32r
I32 = mybir.dt.int32
ALU = mybir.AluOpType
ACT = mybir.ActivationFunctionType
ds = bass.ds

P = 128
SSD_CHUNK = 128
KCONV = 4
KFFN = 3
EPS = 1e-6
MC = 4
GC = MC * P
QC = 4
RING = 4


class Count:

    def __init__(self, eng, sem):
        self.eng, self.sem, self.base, self.n = eng, sem, 0, 0

    def mark(self, ins):
        self.n += 1
        ins.then_inc(self.sem, 1)

    def value(self):
        return self.base + self.n

    def settle(self):
        self.eng.wait_ge(self.sem, self.value())

    def link(self, ins):
        self.mark(ins)
        self.settle()

    def enter(self, i, first, per):
        self.outer, self.per = self.value(), per
        self.base, self.n = (i - first) * per + self.outer, 0

    def leave(self, turns):
        assert self.n == self.per, (self.n, self.per)
        self.base, self.n = self.outer + turns * self.per, 0


class Place:

    KEYS = ("quad", "split", "group", "ada")

    def __init__(self):
        self.base = dict.fromkeys(self.KEYS, 0)
        self.off = dict.fromkeys(self.KEYS, 0)

    @property
    def quad(self):
        return self.base["quad"] + self.off["quad"]

    @property
    def split(self):
        return self.base["split"] + self.off["split"]

    @property
    def group(self):
        return self.base["group"] + self.off["group"]

    @property
    def ada(self):
        return self.base["ada"] + self.off["ada"]

    def step(self, **by):
        for k, v in by.items():
            self.off[k] += v

    def enter(self, i, first, **per):
        self.outer = {k: self.base[k] + self.off[k] for k in self.KEYS}
        self.per = {k: per.get(k, 0) for k in self.KEYS}
        self.base = {k: (i - first) * self.per[k] + self.outer[k] if self.per[k] else self.outer[k] for k in self.KEYS}
        self.off = dict.fromkeys(self.KEYS, 0)

    def leave(self, turns):
        assert self.off == self.per, (self.off, self.per)
        self.base = {k: self.outer[k] + turns * self.per[k] for k in self.KEYS}
        self.off = dict.fromkeys(self.KEYS, 0)


def hybrid_step(nc, x_prompt, x_sample, c_prompt, c_sample, cache_k, cache_v, page_table, state_ssm, state_conv,
                state_ffn_conv, w_ada, b_ada, g_pre_mix, g_post_mix, g_pre_ffn, g_post_ffn, w_in, conv_w, conv_b,
                dt_bias, a_log, d_skip, g_ssd_norm, sb_bias, w_out, w_ffn_in, ffn_conv_w, ffn_conv_b, w_ffn_out,
                y_prompt, y_sample, k_prompt, v_prompt, ssm_prompt, conv_prompt, ffn_conv_prompt,
                k_sample, v_sample, ssm_sample, conv_sample, ffn_conv_sample):
    _, SEQ, DM = x_prompt.shape
    NB, LS, _ = x_sample.shape
    TS = NB * LS
    T = SEQ + TS
    NT = SEQ // P
    KC = DM // P
    _, _, HS, PD, NS = state_ssm.shape
    DSSD = HS * PD
    SC = DSSD // P
    CD = conv_w.shape[2]
    XC = CD // P
    G = (CD - DSSD) // (2 * NS)
    GCH = SC // G
    _, NPOOL, PAGE, HA, DH = cache_k.shape
    DATT = HA * DH
    AC = DATT // P
    NPG = page_table.shape[1]
    DFF = w_ffn_out.shape[1]
    FC = DFF // P
    NSEQ = NB + 1
    MODC = 6 * KC
    SCALE = float(DH) ** -0.5
    ZP, XP, QP, KP, VP = 0, SC, SC + XC, SC + XC + AC, SC + XC + 2 * AC
    PC = SC + XC + 3 * AC
    COL_DT = DSSD + CD
    COL_Q = COL_DT + HS
    ZX_GROUPS = (SC + XC) // MC
    QKV_GROUPS = 3 * AC // MC
    HQ = HA * LS
    assert NT == 2 and TS == 32 and SEQ == 256 and PD == 64 and NS == P and DH == P and PAGE == P
    assert ZX_GROUPS == 5 and QKV_GROUPS == 6 and KC == 16 and FC % MC == 0 and G == 2 and NPG == 8

    ctx = ExitStack()
    with ctx:
        BASE = -(-nc.sbuf_base // 32) * 32
        at = lambda name, shape, off, dt=F32: nc.alloc_sbuf_tensor_at(name, shape, dt, offset=BASE + off)
        CH = T * 4
        raw = at("raw", [P, RING, QC, GC], 0)
        WREG = RING * QC * GC * 4
        whi = at("whi", [P, 2, QC, GC], WREG, F32R)
        wlo = at("wlo", [P, 2, QC, GC], WREG + 16384, F32R)
        cur = [WREG + 32768]

        def keep(name, shape, dt=F32):
            size = 4
            for d in shape[1:]:
                size *= d
            t = at(name, shape, cur[0], dt)
            cur[0] += -(-size // 32) * 32
            return t

        xT = keep("xT", [P, KC, T])
        modT = keep("modT", [P, MODC, NSEQ])
        vecT = keep("vecT", [P, 6, P])
        ctxT = keep("ctxT", [P, 2 * FC, NB * (KFFN - 1)])
        xpad = keep("xpad", [P, XC, NB, LS + KCONV - 1])
        ident = keep("ident", [P, P])
        ones = keep("ones", [P, P])
        incl = keep("incl", [P, P])
        later = keep("later", [P, P])
        cmask = keep("cmask", [P, 3 * P])
        sel = keep("sel", [HS, SC, P])
        zbias = keep("zbias", [P, NPG, HA, LS])
        cT = keep("cT", [P, KC, NSEQ])
        incl_s = keep("incl_s", [TS, TS])
        later_s = keep("later_s", [TS, TS])
        before_s = keep("before_s", [TS, TS])
        seq_of = keep("seq_of", [TS, NB])
        gainT = keep("gainT", [P, KC, NSEQ])
        rT = keep("rT", [P, T])
        ptab = keep("ptab", [1, NB * NPG], I32)
        dtb = keep("dtb", [HS, 1])
        nega = keep("nega", [HS, 1])
        dskip = keep("dskip", [HS, 1])
        sbb = keep("sbb", [P, HA])
        dskE = keep("dskE", [P, SC])
        eps = keep("eps", [P, 1])
        dA_tok = keep("dA_tok", [P, NT + 1, HS])
        ac_tok = keep("ac_tok", [P, NT + 1, HS])
        dend_tok = keep("dend_tok", [P, NT + 2, HS])
        D = cur[0]
        room = nc.sbuf_usable_end - BASE - D
        assert room >= 99840 + CH, room

        hhi = at("hhi", [P, KC, T], D, F32R)
        hlo = at("hlo", [P, KC, T], D + 16 * CH, F32R)
        sq0 = at("sq0", [P, KC, T], D)
        proj = at("proj", [P, PC, T], D + 32 * CH)
        xrow = at("xrow", [P, NT + 1, DM], D + 32 * CH)
        vrow = at("vrow", [P, 6, P], D + 61440)
        crow = at("crow", [NSEQ, DM], D + 64512)
        frow = at("frow", [P, 11, P], D + 72704)
        srow = at("srow", [P, 3, P], D + 78336)
        hf = at("hf", [P, KC, T], D + 32 * CH + KP * CH)
        wdt = at("wdt", [P, KC, HS], D + 87552)
        dtraw = at("dtraw", [HS, T], D + 99840)
        kring = at("kring", [P, 4, HA, DH], D)
        vring = at("vring", [P, 4, HA, DH], D + 16384)
        kstage = at("kstage", [P, DATT], D + 32768)
        vtok = at("vtok", [P, NT + 1, DATT], D + 87552)
        kt = at("kt", [P, 2, HA, P], WREG)
        oT = at("oT", [P, AC, T], WREG + 8192)
        pz, pa, psp, pspm, pw = (at(n, [P, 3 * P], WREG + 17408 + 1536 * i)
                                 for i, n in enumerate(("pz", "pa", "psp", "pspm", "pw")))
        o_new = at("o_new", [P, HA, TS], WREG + 25088)
        dz, da, dsp, dw = (at(n, [P, NPG, HA, LS], WREG + 26624 + 1024 * i)
                           for i, n in enumerate(("dz", "da", "dsp", "dw")))
        ccol = at("ccol", [P, 3, 27, 4], WREG + 26624)
        cout = at("cout", [27 * 4, 3, P], WREG + 26624 + 1536)
        qb = at("qb", [P, HA, LS], WREG + 30720)
        sp_new = at("sp_new", [TS, HA, TS], WREG + 30848)
        xc = at("xc", [P, XC, T], D)
        xdt_tok = at("xdt_tok", [P, NT + 1, DSSD], D + 13824)
        xdtT = at("xdtT", [P, SC, T], D + 26112)
        xde_s = at("xde_s", [TS, DSSD], D + 26112)
        B_tok = at("B_tok", [P, NT + 1, G, NS], D + 30208)
        yoff_s = at("yoff_s", [P, SC, TS], D + 35328)
        xde = at("xde", [P, 3, DSSD], D + 46080)
        yT = at("yT", [P, SC, T], D + 59904)
        ohi = at("ohi", [P, AC, T], D + 69120, F32R)
        olo = at("olo", [P, AC, T], D + 78336, F32R)
        h0 = at("h0", [P, 2, SC, NS], D + 87552)
        h0T = at("h0T", [P, SC, P], D + 95744)
        hb = at("hb", [HS, HS, P], WREG)
        hnew = at("hnew", [P, 2, SC, NS], WREG)
        eaE = at("eaE", [P, SC, P + TS], WREG + 8192)
        cbm = at("cbm", [P, G, T], WREG + 13312)
        seg = at("seg", [P, 2, T], WREG + 15616)
        dec = at("dec", [P, 2, T], WREG + 17920)
        sco = at("sco", [P, 2, T], WREG + 20224)
        h1T = at("h1T", [P, DSSD], WREG + 22528)
        dtT, dA_T, acT, t1, t2 = (at(n, [HS, T], WREG + 26624 + CH * i)
                                  for i, n in enumerate(("dtT", "dA_T", "acT", "t1", "t2")))
        bm_s = at("bm_s", [TS, G, NS], D + 33280)
        ctmp = at("ctmp", [P, XC, TS], D + 13824)
        ytmp = at("ytmp", [P, SC, P], WREG + 15616)
        rg = at("rg", [P, G, T], WREG + 22528)
        sq1 = at("sq1", [P, SC, T], D + 46080)
        yhi = at("yhi", [P, SC, T], D, F32R)
        ylo = at("ylo", [P, SC, T], D + SC * CH, F32R)
        mT = at("mT", [P, KC, T], D + 16 * CH)
        sq2 = at("sq2", [P, KC, T], D + 32 * CH)
        h2f = at("h2f", [P, KC, T], D + 48 * CH)
        h2hi = at("h2hi", [P, KC, T], D, F32R)
        h2lo = at("h2lo", [P, KC, T], D + 16 * CH, F32R)
        fT = at("fT", [P, KC, T], D + 32 * CH)
        UP = SEQ + KFFN - 1 + NB * (LS + KFFN - 1)
        ghi = at("ghi", [P, MC, T], D + 55296, F32R)
        glo = at("glo", [P, MC, T], D + 59904, F32R)
        fw = at("fw", [P, 4, 2, MC], D + 64512)
        ug = at("ug", [P, MC, UP], D + 73728)
        uv = at("uv", [P, MC, UP], D + 78624)
        cg = at("cg", [P, MC, UP], D + 83520)
        cv = at("cv", [P, MC, UP], D + 88416)
        pcol = at("pcol", [P, 2 * FC, 2], D + 93312)
        gt = at("gt", [P, MC, T], D + 94016)
        fcomp = at("fcomp", [P, 11, P], D + 55296)
        sq3 = at("sq3", [P, KC, T], D)
        ystage = at("ystage", [P, NT + 1, DM], D + 55296)
        fstage = at("fstage", [P, 11, P], D + 79872)
        fpstage = at("fpstage", [2 * FC, 2, P], D + 85504)

        ps = ctx.enter_context(nc.psum_tensor("ps", [P, 8, 512], F32))

        def sem(name):
            return ctx.enter_context(nc.semaphore(name))

        raw_full = [sem(f"raw_full{j}") for j in range(RING)]
        hi_ready, lo_ready, w_used, ada_used = sem("hi_ready"), sem("lo_ready"), sem("w_used"), sem("ada_used")
        group_free, ada_free = sem("group_free"), sem("ada_free")
        in_c, in_vec, in_ctx, in_x, in_misc, in_pt = (sem(n) for n in ("in_c", "in_vec", "in_ctx", "in_x", "in_misc", "in_pt"))
        consts = sem("consts")
        pool_c, act_c, dve_c = sem("pool_c"), sem("act_c"), sem("dve_c")
        rows_T = sem("rows_T")
        rows_out = sem("rows_out")
        x_T, x_out = sem("x_T"), sem("x_out")
        c_ready = sem("c_ready")
        sq_ready, sum_ready, root_ready, r_ready = sem("sq_ready"), sem("sum_ready"), sem("root_ready"), sem("r_ready")
        xr_ready, gain_ready, hp_ready, hs_ready = sem("xr_ready"), sem("gain_ready"), sem("hp_ready"), sem("hs_ready")
        h_hi, h_lo = sem("h_hi"), sem("h_lo")
        dt_full, dt_out = sem("dt_full"), sem("dt_out")
        tok_full, ktok_out, vtok_out, tok_dma = sem("tok_full"), sem("ktok_out"), sem("vtok_out"), sem("tok_dma")
        ccol_ready, ccol_T, ccol_out, ccol_dma = sem("ccol_ready"), sem("ccol_T"), sem("ccol_out"), sem("ccol_dma")
        xpad_ready = sem("xpad_ready")
        z_full, z_e, z_sp, tail_full, w_e, w_ready, o_full, o_out = (
            sem(n) for n in ("z_full", "z_e", "z_sp", "tail_full", "w_e", "w_ready", "o_full", "o_out"))
        z_na = sem("z_na")
        w_d = sem("w_d")
        kfull = [sem(f"kfull{j}") for j in range(4)]
        vfull = [sem(f"vfull{j}") for j in range(4)]
        kT_full, kT_act, kT_dve = sem("kT_full"), sem("kT_act"), sem("kT_dve")
        qb_ready, page_scored, page_summed = sem("qb_ready"), sem("page_scored"), sem("page_summed")
        dn_na, dn_e, dn_sp, dtail_full, dn_d, dn_w, do_out = (
            sem(n) for n in ("dn_na", "dn_e", "dn_sp", "dtail_full", "dn_d", "dn_w", "do_out"))
        ov_hi, ov_lo = sem("ov_hi"), sem("ov_lo")
        conv_done, silu_done = sem("conv_done"), sem("silu_done")
        a2d, d2a, d2p, p2d, p2a, a2p, g2 = (sem(n) for n in ("a2d", "d2a", "d2p", "p2d", "p2a", "a2p", "g2"))
        hb_ready = sem("hb_ready")
        bc_full, seg_ready, dec_ready, sco_ready, yd_full, yd_out = (
            sem(n) for n in ("bc_full", "seg_ready", "dec_ready", "sco_ready", "yd_full", "yd_out"))
        h0_full = [sem(f"h0_full{j}") for j in range(2)]
        h0T_full, h0T_out, bm_ready, hn_full, hn_out, ys_full, ys_out = (
            sem(n) for n in ("h0T_full", "h0T_out", "bm_ready", "hn_full", "hn_out", "ys_full", "ys_out"))
        hn_dma = [sem(f"hn_dma{j}") for j in range(2)]
        y_hi, y_lo = sem("y_hi"), sem("y_lo")
        x2_ready = sem("x2_ready")
        f_u, f_c, f_s, f_gt, f_hi, f_lo, f_ctx, f_col, f_fw = (
            sem(n) for n in ("f_u", "f_c", "f_s", "f_gt", "f_hi", "f_lo", "f_ctx", "f_col", "f_fw"))
        fcomp_ready = sem("fcomp_ready")
        ys_T, ys_o, out_dma = sem("ys_T"), sem("ys_o"), sem("out_dma")
        fc_T, fc_o = sem("fc_T"), sem("fc_o")
        (dt_na, dt_e, dt_ln, dt_done, a_ready, dA_full, dA_ready, ac_full, ac_out, ac_exp, xdt_made, dtE_full, eaE_made,
         acE_full, xdt_full, xdt_out, B_full, B_out, cb_full, cbm_made, xde_made, h1_full, h1_out, yo_full, yo_out,
         z_silu, y_gated, ysq_ready, y_normed, f_add) = (
            sem(n) for n in ("dt_na", "dt_e", "dt_ln", "dt_done", "a_ready", "dA_full", "dA_ready", "ac_full", "ac_out",
                             "ac_exp", "xdt_made", "dtE_full", "eaE_made", "acE_full", "xdt_full", "xdt_out", "B_full",
                             "B_out", "cb_full", "cbm_made", "xde_made", "h1_full", "h1_out", "yo_full", "yo_out",
                             "z_silu", "y_gated", "ysq_ready", "y_normed", "f_add"))
        ssm_dma, ssm_full, ssm_out = sem("ssm_dma"), sem("ssm_full"), sem("ssm_out")

        w_ada_v, w_in_v, w_out_v, w_fi_v, w_fo_v = w_ada[0], w_in[0], w_out[0], w_ffn_in[0], w_ffn_out[0]

        SH1, SC1, G1, SH2, SC2, G2 = (k * KC for k in range(6))
        V_PRE_MIX, V_POST_MIX = (0, MODC), (0, MODC + KC)
        V_PRE_FFN, V_POST_FFN = (1, 0), (1, KC)
        V_CW, V_CB, V_GS = 2 * KC, 2 * KC + KCONV * XC, 2 * KC + (KCONV + 1) * XC

        def smp(ap):
            return ap[:, :, SEQ:T].rearrange("p n (b t) -> p n b t", b=NB)

        block = ctx.enter_context(nc.Block())

        @block.sync
        def _(sp):
            pos = Place()
            last = [None]

            def free(j):
                if last[0] == "G":
                    sp.wait_ge(lo_ready, 4 * (pos.split - 1) + j + 1)
                elif last[0] == "a":
                    sp.wait_ge(ada_used, 4 * (pos.ada - 1) + j + 1)

            def quad(kind, src):
                for j in range(RING):
                    free(j)
                    sp.dma_start(raw[:, j], src(j)).then_inc(raw_full[j], 16)
                last[0] = kind
                pos.step(quad=1, **({"split": 1} if kind == "G" else {"ada": 1}))

            def rows(w, j, col):
                return w[j * QC * P:(j + 1) * QC * P, ds(col, GC)].rearrange("(q p) n -> p q n", p=P)

            def ada():
                quad("a", lambda j: rows(w_ada_v, j, pos.ada * GC))

            def proj_in(col):
                quad("G", lambda j: rows(w_in_v, j, col))

            quad("a", lambda j: rows(w_ada_v, j, 0))
            with sp.Fori(1, 8) as i:
                pos.enter(i, 1, quad=1, ada=1)
                ada()
                pos.leave(7)
            proj_in(0)
            ada()
            with sp.Fori(0, 2) as i:
                pos.enter(i, 0, quad=4, split=2, ada=2)
                for half in range(2):
                    proj_in(i * (2 * GC) + (half + 1) * GC)
                    ada()
                pos.leave(2)
            with sp.Fori(0, 3) as i:
                pos.enter(i, 0, quad=4, split=2, ada=2)
                for half in range(2):
                    proj_in(i * (2 * GC) + half * GC + COL_Q)
                    ada()
                pos.leave(3)

            sp.wait_ge(w_used, 4 * (ZX_GROUPS + QKV_GROUPS))
            sp.wait_ge(in_pt, 16)

            def k_page(b, p):
                if not (isinstance(b, int) and b * NPG + p < 4):
                    sp.wait_ge(kT_full, b * NPG + p - 3)
                pg = sp.value_load(ptab[0:1, ds(b * NPG + p, 1)], min_val=0, max_val=NPOOL - 1)
                sp.dma_start(kring[:, p % 4], cache_k[0][ds(pg, 1)].rearrange("o k h d -> (o k) h d"))\
                    .then_inc(kfull[p % 4], 16)

            def v_page(b, p):
                if not (isinstance(b, int) and b * NPG + p < 4):
                    sp.wait_ge(page_summed, b * NPG + p - 3)
                pg = sp.value_load(ptab[0:1, ds(b * NPG + p, 1)], min_val=0, max_val=NPOOL - 1)
                sp.dma_start(vring[:, p % 4], cache_v[0][ds(pg, 1)].rearrange("o k h d -> (o k) h d"))\
                    .then_inc(vfull[p % 4], 16)

            for p in range(NPG):
                k_page(0, p)
            for p in range(NPG):
                k_page(1, p)
                v_page(0, p)
            with sp.Fori(2, NB) as b:
                for p in range(NPG):
                    k_page(b, p)
                    v_page(b - 1, p)
            for p in range(NPG):
                v_page(NB - 1, p)

            sp.wait_ge(o_out, 1 + HA)
            sp.wait_ge(tok_dma, 16 * 6)
            for b in range(NB):
                if b >= 2:
                    sp.wait_ge(hn_out, b - 1)
                sp.dma_start(h0[:, b % 2], state_ssm[0, b].rearrange("(c a) d n -> (a d) c n", a=P // PD))\
                    .then_inc(h0_full[b % 2], 16)

            with sp.Fori(0, 2) as i:
                pos.enter(i, 0, quad=4, split=2, ada=2)
                for half in range(2):
                    quad("G", lambda j: rows(w_out_v, j, i * (2 * GC) + half * GC))
                    ada()
                pos.leave(2)
            ada()

            def fo(r):
                def src(n):
                    return w_fo_v[ds(r * GC, GC), n * GC:(n + 1) * GC].rearrange("(q p) n -> p q n", p=P)
                quad("G", src)

            def round_(r, out):
                quad("G", lambda j: rows(w_fi_v, j, r * GC))
                quad("G", lambda j: rows(w_fi_v, j, r * GC + DFF))
                if out:
                    fo(r - 1)

            round_(0, False)
            round_(1, True)
            with sp.Fori(2, FC // MC) as r:
                pos.enter(r, 2, quad=3, split=3)
                round_(r, True)
                pos.leave(FC // MC - 2)
            fo(FC // MC - 1)

        @block.gpsimd
        def _(pool):
            c = Count(pool, pool_c)
            ge, fill = ALU.is_ge, 0.0
            for m, v in ((ident, 0.0), (ones, 1.0), (incl, 1.0), (later, 1.0), (cmask, 1.0), (sel, 1.0), (incl_s, 1.0),
                         (later_s, 1.0), (before_s, 1.0), (seq_of, 1.0)):
                c.mark(pool.memset(m[:], v))
            c.settle()

            def keep_where(m, pattern, base, cm):
                c.mark(pool.affine_select(out=m, in_=m, compare_op=ge, fill=fill, base=base, pattern=pattern,
                                          channel_multiplier=cm))

            c.mark(pool.affine_select(out=ident[:], in_=ident[:], compare_op=ALU.not_equal, fill=1.0, base=0,
                                      pattern=[[-1, P]], channel_multiplier=1))
            keep_where(incl[:], [[1, P]], 0, -1)
            keep_where(later[:], [[-1, P]], -1, 1)
            keep_where(cmask[:, 0:P], [[1, P]], -1, -1)
            keep_where(cmask[:, 2 * P:3 * P], [[1, P]], -1, -1)
            keep_where(sel[:], [[P, SC], [1, P]], 0, -PD)
            keep_where(incl_s[:], [[1, TS]], 0, -1)
            keep_where(later_s[:], [[-1, TS]], -1, 1)
            keep_where(before_s[:], [[1, TS]], -1, -1)
            keep_where(seq_of[:], [[-LS, NB]], 0, 1)
            c.settle()
            keep_where(sel[:], [[-P, SC], [-1, P]], PD - 1, PD)
            keep_where(incl_s[:], [[-LS, NB], [0, LS]], 0, 1)
            keep_where(later_s[:], [[-LS, NB], [0, LS]], 0, 1)
            keep_where(before_s[:], [[-LS, NB], [0, LS]], 0, 1)
            keep_where(seq_of[:], [[LS, NB]], LS - 1, -1)
            c.settle()
            keep_where(incl_s[:], [[LS, NB], [0, LS]], LS - 1, -1)
            keep_where(later_s[:], [[LS, NB], [0, LS]], LS - 1, -1)
            keep_where(before_s[:], [[LS, NB], [0, LS]], LS - 1, -1)
            c.settle()
            c.link(pool.memset(eps[:], EPS))
            pool.memset(dA_tok[:], 0.0).then_inc(consts, 1)
            pool.memset(ac_tok[:], 0.0).then_inc(consts, 1)

            for n in range(2 * (NT + 1)):
                kind, t = divmod(n, NT + 1)
                src = kstage if kind == 0 else vtok
                pool.wait_ge((ktok_out, vtok_out)[kind], t + 1)
                if t < NT:
                    dst = (k_prompt, v_prompt)[kind][0, 0, t * P:(t + 1) * P].rearrange("t h d -> t (h d)")
                    piece = src[:, :] if kind == 0 else src[:, t, :]
                else:
                    dst = (k_sample, v_sample)[kind][0].rearrange("b t h d -> (b t) (h d)")
                    piece = src[0:TS, :] if kind == 0 else src[0:TS, t, :]
                pool.dma_start(dst, piece).then_inc(tok_dma, 16)
            pool.wait_ge(ccol_out, 1)
            pool.dma_start(conv_prompt[0, 0].rearrange("r (g x) -> (r g) x", g=4),
                           cout[0:12].rearrange("p c f -> p (c f)")).then_inc(ccol_dma, 16)
            pool.dma_start(conv_sample[0].rearrange("b r (g x) -> (b r g) x", g=4),
                           cout[12:108].rearrange("p c f -> p (c f)")).then_inc(ccol_dma, 16)

            for b in range(NB):
                if b:
                    pool.wait_ge(page_scored, NPG * b)
                pool.tensor_copy(qb[:], proj[:, QP:QP + AC, SEQ + LS * b:SEQ + LS * (b + 1)]).then_inc(qb_ready, 1)

            pool.wait_ge(ov_lo, 1)
            c.link(pool.memset(hb[:], 0.0))
            c.link(pool.affine_select(out=hb[:], in_=hb[:], compare_op=ALU.not_equal, fill=1.0, base=0,
                                      pattern=[[-1, HS], [0, P]], channel_multiplier=1))
            pool.memset(cbm[:], 0.0).then_inc(hb_ready, 1)

            pool.wait_ge(ssm_out, 1)
            pool.dma_start(ssm_prompt[0, 0].rearrange("(c a) d n -> (a d) c n", a=P // PD), hnew[:, 1]).then_inc(ssm_dma, 16)
            for b in range(NB):
                pool.wait_ge(hn_out, b + 1)
                pool.dma_start(ssm_sample[0, b].rearrange("(c a) d n -> (a d) c n", a=P // PD), hnew[:, b % 2])\
                    .then_inc(hn_dma[b % 2], 16)

            pool.wait_ge(h_lo, 2)
            for u in (ug, uv):
                c.mark(pool.memset(u[:, :, 0:KFFN - 1], 0.0))
            pool.memset(fT[:], 0.0).then_inc(g2, 1)
            c.settle()

            def upad(u, a, n):
                return u[:, :, SEQ + 2:UP].rearrange("p m (b t) -> p m b t", b=NB)[:, :, :, a:a + n]

            def contexts(r, first):
                for s, u in ((0, ug), (1, uv)):
                    chunks = ds(r * MC + s * FC, MC)
                    if not first:
                        pool.wait_ge(f_c, 2 * (r - 1) + s + 1)
                    pool.tensor_copy(upad(u, 0, 2), ctxT[:, chunks, :].rearrange("p m (b t) -> p m b t", b=NB))\
                        .then_inc(f_ctx, 1)
                for s, u in ((0, ug), (1, uv)):
                    chunks = ds(r * MC + s * FC, MC)
                    pool.wait_ge(f_u, 2 * r + s + 1)
                    pool.wait_ge(f_ctx, 2 * r + s + 1)
                    c.mark(pool.tensor_copy(ctxT[:, chunks, :].rearrange("p m (b t) -> p m b t", b=NB), upad(u, LS, 2)))
                    pool.tensor_copy(pcol[:, chunks, :], u[:, :, SEQ:SEQ + 2]).then_inc(f_col, 1)

            for r in range(FC // MC):
                contexts(r, r == 0)

            c.settle()
            pool.wait_ge(f_lo, FC // MC)
            pool.wait_ge(w_used, 4 * (ZX_GROUPS + QKV_GROUPS + 4 + 3 * FC // MC))
            pool.tensor_copy(fcomp[:].rearrange("p c (r g) -> p c r g", g=8),
                             ctxT[:].rearrange("p (g c) r -> p c r g", c=11)).then_inc(fcomp_ready, 1)
            pool.wait_ge(fc_o, 2)
            pool.dma_start(ffn_conv_sample[0].rearrange("b r (g x) -> (b r g) x", g=8),
                           fstage[:].rearrange("p c f -> p (c f)")).then_inc(out_dma, 16)
            for r in range(2):
                pool.dma_start(ffn_conv_prompt[0, 0, r].rearrange("(c f) -> c f", f=P), fpstage[:, r]).then_inc(out_dma, 16)
            for t in range(NT):
                pool.wait_ge(ys_o, 4 * (t + 1))
                pool.dma_start(y_prompt[0, t * P:(t + 1) * P], ystage[:, t]).then_inc(out_dma, 16)
            pool.wait_ge(ys_o, 4 * (NT + 1))
            pool.dma_start(y_sample.rearrange("b t d -> (b t) d"), ystage[0:TS, NT]).then_inc(out_dma, 16)
            pool.wait_ge(out_dma, 16 * 6)
            pool.wait_ge(tok_dma, 16 * 6)
            pool.wait_ge(ccol_dma, 32)
            pool.wait_ge(ssm_dma, 16)
            pool.wait_ge(hn_dma[0], 16 * (NB // 2))
            pool.wait_ge(hn_dma[1], 16 * (NB // 2))

        @block.tensor
        def _(pe):
            pos = Place()
            mm = nc.tensor.matmul

            def tr(out, in_, k):
                return nc.tensor.transpose(out, in_, ident[0:k, 0:k])

            def adaq(bank):
                pe.wait_ge(group_free, pos.group + 1)
                if not isinstance(pos.ada, int) or pos.ada > 0:
                    pe.wait_ge(ada_free, pos.ada)
                for j in range(RING):
                    pe.wait_ge(raw_full[j], 16 * (pos.quad + 1))
                    for q in range(QC):
                        for m in range(MC):
                            i = mm(ps[:, bank, m * NSEQ:(m + 1) * NSEQ], raw[:, j, q, m * P:(m + 1) * P],
                                   cT[:, j * QC + q, :], start=(j + q + m == 0), stop=(j + 1, q + 1, m + 1) == (RING, QC, MC),
                                   skip_group_check=True)
                    i.then_inc(ada_used, 1)
                pos.step(quad=1, ada=1)

            def unit3(j, bank0, xs, first, last):
                s = j % 2
                for q in range(QC):
                    xh, xl = xs(q)
                    for m in range(MC):
                        o = ps[:, bank0 + m, 0:T]
                        cols = slice(m * P, (m + 1) * P)
                        mm(o, whi[:, s, q, cols], xh, start=(first and q == 0), stop=False)
                        mm(o, whi[:, s, q, cols], xl, start=False, stop=False)
                        i = mm(o, wlo[:, s, q, cols], xh, start=False, stop=(last and q == QC - 1))
                return i

            def group(bank0, xhi, xlo):
                pe.wait_ge(group_free, pos.group + 1)
                pe.wait_ge(ada_free, pos.ada)
                for j in range(RING):
                    pe.wait_ge(lo_ready, 4 * pos.split + j + 1)
                    i = unit3(j, bank0, lambda q: (xhi(j * QC + q), xlo(j * QC + q)), j == 0, j == RING - 1)
                    i.then_inc(w_used, 1)
                pos.step(quad=1, split=1, group=1)

            pe.wait_ge(pool_c, 28)
            pe.wait_ge(in_vec, 16 * 10)
            for n in range(6):
                k = P if n == 0 else (2 * KC + (KCONV + 1) * XC + SC if n == 1 else 2 * FC)
                i = tr(ps[:, n // 4, (n % 4) * P:(n % 4) * P + k], vrow[0:k, n, :], k)
            i.then_inc(rows_T, 1)
            pe.wait_ge(in_c, 32)
            for k in range(KC):
                i = tr(ps[:, 1, 256 + k * NSEQ:256 + (k + 1) * NSEQ], crow[:, k * P:(k + 1) * P], NSEQ)
            i.then_inc(rows_T, 1)
            pe.wait_ge(in_ctx, 32)
            for n in range(11):
                i = tr(ps[:, 2 + n // 4, (n % 4) * P:(n % 4 + 1) * P], frow[:, n, :], P)
            i.then_inc(rows_T, 1)
            for n in range(3):
                i = tr(ps[:, 5, n * 96:(n + 1) * 96], srow[0:96, n, :], 96)
            i.then_inc(rows_T, 1)
            pe.wait_ge(in_x, 48)
            for n in range(12):
                t, g = divmod(n, 4)
                k = P if t < NT else TS
                if n == 2:
                    pe.wait_ge(rows_out, 1)
                    pe.wait_ge(c_ready, 1)
                if n >= 8:
                    pe.wait_ge(x_out, n - 7)
                for m in range(4):
                    c0 = (g * 4 + m) * P
                    i = tr(ps[:, (6 + n) % 8, m * k:(m + 1) * k], xrow[0:k, t, c0:c0 + P], k)
                i.then_inc(x_T, 1)

            norms = [0]

            def sums(sq, chunks, bank):
                for n, k in enumerate(chunks):
                    i = mm(ps[:, bank, 0:T], ones[:], sq[:, k, :], start=(n == 0), stop=(n == len(chunks) - 1))
                i.then_inc(sum_ready, 1)

            def norm_sums(sq):
                norms[0] += 1
                pe.wait_ge(sq_ready, norms[0])
                sums(sq, range(KC), 2)

            pe.wait_ge(x_out, 12)
            norm_sums(sq0)
            pe.wait_ge(c_ready, 1)
            adaq(4)
            with pe.Fori(1, 8) as i_:
                pos.enter(i_, 1, quad=1, ada=1)
                adaq(4)
                pos.leave(7)

            pe.wait_ge(in_misc, 16 * 5)
            pe.wait_ge(hp_ready, 1)
            pe.wait_ge(hs_ready, 1)
            for k in range(KC):
                i = mm(ps[0:HS, 7, 0:T], wdt[:, k, :], hf[:, k, :], start=(k == 0), stop=(k == KC - 1))
            i.then_inc(dt_full, 1)
            pe.wait_ge(h_lo, 1)
            pe.wait_ge(dt_out, 1)

            def pair(bank0, xh, xl):
                group(bank0, xh, xl)
                adaq(4 - bank0)

            def pairs(turns, bank0, xh, xl):
                with pe.Fori(0, turns) as i_:
                    pos.enter(i_, 0, quad=4, split=2, group=2, ada=2)
                    pair(bank0, xh, xl)
                    pair(4 - bank0, xh, xl)
                    pos.leave(turns)

            hx = (lambda k: hhi[:, k, :]), (lambda k: hlo[:, k, :])
            pair(0, *hx)
            pairs(2, 4, *hx)
            pairs(3, 4, *hx)

            pe.wait_ge(group_free, 2 + ZX_GROUPS + QKV_GROUPS)
            pe.wait_ge(ada_free, 8 + ZX_GROUPS + QKV_GROUPS)
            for n in range(2 * (NT + 1)):
                kind, t = divmod(n, NT + 1)
                w = P if t < NT else TS
                if n >= 2:
                    pe.wait_ge((ktok_out, vtok_out)[(n - 2) // 3], (n - 2) % 3 + 1)
                for h in range(HA):
                    i = tr(ps[0:w, 2 * (n % 2) + h // 4, (h % 4) * P:(h % 4 + 1) * P],
                           proj[:, (KP, VP)[kind] + h, t * P:t * P + w], P)
                i.then_inc(tok_full, 1)
            pe.wait_ge(ccol_ready, 1)
            for c in range(3):
                i = tr(ps[0:108, 7, c * P:(c + 1) * P], ccol[:, c].rearrange("p r g -> p (r g)"), P)
            i.then_inc(ccol_T, 1)

            for h in range(HA):
                i = mm(ps[0:TS, 4, h * TS:(h + 1) * TS], proj[:, KP + h, SEQ:T], proj[:, QP + h, SEQ:T],
                       start=True, stop=True)
            i.then_inc(z_full, 1)
            pe.wait_ge(z_sp, 1)
            mm(ps[0:TS, 5, 0:HA * TS], later[0:TS, 0:TS], sp_new[:].rearrange("p h t -> p (h t)"), start=True, stop=True)\
                .then_inc(tail_full, 1)
            pe.wait_ge(w_ready, 1)
            pe.wait_ge(vtok_out, 3)
            for h in range(HA):
                i = mm(ps[:, 6, h * TS:(h + 1) * TS], vtok[0:TS, NT, h * DH:(h + 1) * DH], pa[0:TS, h * TS:(h + 1) * TS],
                       start=True, stop=True)
            i.then_inc(o_full, 1)

            def scores(h):
                z = ps[:, h % 2]
                mm(z[:, 0:2 * P], proj[:, KP + h, 0:P], proj[:, QP + h, 0:2 * P], start=True, stop=True)
                mm(z[:, 2 * P:3 * P], proj[:, KP + h, P:2 * P], proj[:, QP + h, P:2 * P], start=True, stop=True)\
                    .then_inc(z_full, 1)

            for h in range(2):
                scores(h)
            for h in range(HA):
                tail = ps[:, 2 + h % 2]
                pe.wait_ge(z_sp, h + 2)
                mm(tail[:, 0:3 * P], later[:], pspm[:], start=True, stop=True)
                mm(tail[:, P:2 * P], ones[:], pspm[:, 2 * P:3 * P], start=False, stop=True, skip_group_check=True)\
                    .then_inc(tail_full, 1)
                pe.wait_ge(w_ready, h + 2)
                if h >= 2:
                    pe.wait_ge(o_out, h)
                o = ps[:, 4 + h % 2]
                mm(o[:, 0:2 * P], vtok[:, 0, h * DH:(h + 1) * DH], pw[:, 0:2 * P], start=True, stop=True)
                mm(o[:, P:2 * P], vtok[:, 1, h * DH:(h + 1) * DH], pw[:, 2 * P:3 * P], start=False, stop=True,
                   skip_group_check=True).then_inc(o_full, 1)
                if h + 2 < HA:
                    scores(h + 2)

            pe.wait_ge(o_out, 1 + HA)
            pe.wait_ge(ccol_out, 1)

            def page_T(b, p, n):
                pe.wait_ge(kfull[p % 4], 16 * (2 * b + p // 4 + 1))
                if not (isinstance(n, int) and n < 2):
                    pe.wait_ge(kT_act, n - 1)
                    pe.wait_ge(kT_dve, n - 1)
                for h in range(HA):
                    i = tr(ps[:, 2 * (p % 2) + h // 4, (h % 4) * P:(h % 4 + 1) * P], kring[:, p % 4, h, :], P)
                i.then_inc(kT_full, 1)

            def page_scores(b, p, n):
                pe.wait_ge(kT_act, n + 1)
                pe.wait_ge(kT_dve, n + 1)
                if p == 0:
                    pe.wait_ge(qb_ready, b + 1)
                    if not (isinstance(b, int) and b == 0):
                        pe.wait_ge(dn_na, b)
                for h in range(HA):
                    c0 = (p * HA + h) * LS
                    i = mm(ps[:, 4, c0:c0 + LS], kt[:, p % 2, h, :], qb[:, h, :], start=True, stop=True)
                i.then_inc(page_scored, 1)

            def tails(b):
                pe.wait_ge(dn_sp, b + 1)
                mm(ps[:, 6, 0:NPG * HQ], later[:], dsp[:].rearrange("p g h t -> p (g h t)"), start=True, stop=True)
                for p in range(1, NPG):
                    mm(ps[:, 6, 0:p * HQ].rearrange("p (g x) -> p g x", g=p), ones[:],
                       dsp[:, p].rearrange("p h t -> p (h t)").unsqueeze(1).to_broadcast([P, p, HQ]),
                       start=False, stop=True, skip_group_check=True)
                for p in range(NPG):
                    i = mm(ps[:, 6, p * HQ:(p + 1) * HQ].rearrange("p (h t) -> p h t", h=HA), ones[0:TS, :],
                           sp_new[:, :, ds(b * LS, LS)], start=False, stop=True, skip_group_check=True)
                i.then_inc(dtail_full, 1)

            def page_sum(b, p):
                pe.wait_ge(vfull[p % 4], 16 * (2 * b + p // 4 + 1))
                if p == 0:
                    pe.wait_ge(dn_w, b + 1)
                    if not (isinstance(b, int) and b == 0):
                        pe.wait_ge(do_out, b)
                for h in range(HA):
                    i = mm(ps[:, 5, h * LS:(h + 1) * LS], vring[:, p % 4, h, :], dw[:, p, h, :],
                           start=(p == 0 and h == 0), stop=(p + 1, h + 1) == (NPG, HA), skip_group_check=True)
                i.then_inc(page_summed, 1)

            def sequence(b):
                n = b * NPG
                first = isinstance(b, int) and b == 0
                page_T(b, 0, n)
                page_T(b, 1, n + 1)
                page_scores(b, 0, n)
                if not first:
                    tails(b - 1)
                for p in range(2, NPG):
                    page_T(b, p, n + p)
                    page_scores(b, p - 1, n + p - 1)
                    if not first:
                        for v in {3: [0], 4: [1], 5: [2, 3], 6: [4, 5], 7: [6, 7]}.get(p, []):
                            page_sum(b - 1, v)
                page_scores(b, NPG - 1, n + NPG - 1)

            sequence(0)
            sequence(1)
            with pe.Fori(2, NB) as b:
                sequence(b)
            tails(NB - 1)
            for p in range(NPG):
                page_sum(NB - 1, p)

            pe.wait_ge(do_out, NB)
            pe.wait_ge(dt_done, 1)
            for t in range(NT + 1):
                w = P if t < NT else TS
                i = tr(ps[0:w, 0, t * HS:(t + 1) * HS], dA_T[:, t * P:t * P + w], HS)
            i.then_inc(dA_full, 1)
            pe.wait_ge(dA_ready, 1)
            for t in range(NT):
                mm(ps[:, 1, t * HS:(t + 1) * HS], incl[:], dA_tok[:, t, :], start=True, stop=True)
                mm(ps[0:HS, 2, t * P:(t + 1) * P], dA_tok[:, t, :], incl[:], start=True, stop=True)
            mm(ps[0:TS, 1, NT * HS:(NT + 1) * HS], incl_s[:], dA_tok[0:TS, NT, :], start=True, stop=True)
            mm(ps[0:HS, 2, SEQ:T], dA_tok[0:TS, NT, :], incl_s[:], start=True, stop=True)
            mm(ps[:, 3, 0:HS], later[:], dA_tok[:, 0, :], start=True, stop=True)
            mm(ps[:, 3, HS:2 * HS], later[:], dA_tok[:, 0, :], start=True, stop=False)
            mm(ps[:, 3, HS:2 * HS], ones[:], dA_tok[:, 1, :], start=False, stop=True)
            mm(ps[:, 3, 2 * HS:3 * HS], later[:], dA_tok[:, 1, :], start=True, stop=True)
            mm(ps[0:TS, 3, 3 * HS:4 * HS], later_s[:], dA_tok[0:TS, NT, :], start=True, stop=True)
            for c in range(SC):
                i = mm(ps[:, 4, c:c + 1], sel[:, c, :], dskip[:], start=True, stop=True)
            i.then_inc(ac_full, 1)
            pe.wait_ge(ac_out, 1)
            pe.wait_ge(ac_exp, 1)
            for c in range(SC):
                if c >= 2:
                    pe.wait_ge(xdt_made, c - 1)
                mm(ps[:, 4 + c % 2, 0:T], sel[:, c, :], dtT[:], start=True, stop=True).then_inc(dtE_full, 1)
                if c >= 2:
                    pe.wait_ge(eaE_made, c - 1)
                mm(ps[:, 6 + c % 2, 0:P + TS], sel[:, c, :], acT[:, P:T], start=True, stop=True).then_inc(acE_full, 1)
            pe.wait_ge(xdt_made, SC)
            for t in range(NT + 1):
                w = P if t < NT else TS
                if t == 2:
                    pe.wait_ge(xdt_out, 1)
                for c in range(SC):
                    i = tr(ps[0:w, 2 * (t % 2) + c // 4, (c % 4) * P:(c % 4 + 1) * P], xdtT[:, c, t * P:t * P + w], P)
                i.then_inc(xdt_full, 1)
            pe.wait_ge(eaE_made, SC)
            for t in range(NT + 1):
                w = P if t < NT else TS
                for g in range(G):
                    i = tr(ps[0:w, 4 + t // 2, (t % 2) * G * NS + g * NS:(t % 2) * G * NS + (g + 1) * NS],
                           xc[:, SC + g, t * P:t * P + w], P)
            i.then_inc(B_full, 1)
            for g in range(G):
                for t in range(NT + 1):
                    w = P if t < NT else TS
                    i = mm(ps[0:w, 6 + g, t * P:t * P + w], xc[:, SC + g, t * P:t * P + w],
                           xc[:, SC + G + g, t * P:t * P + w], start=True, stop=True)
            i.then_inc(cb_full, 1)

            pe.wait_ge(B_out, 1)
            pe.wait_ge(xde_made, 1)
            pe.wait_ge(xdt_out, 3)
            for g in range(G):
                i = mm(ps[:, g, :], B_tok[:, 0, g, :], xde[:, 0, g * GCH * P:(g + 1) * GCH * P], start=True, stop=True)
            i.then_inc(h1_full, 1)

            pe.wait_ge(cbm_made, 1)
            pe.wait_ge(hb_ready, 1)
            pe.wait_ge(h1_out, 1)

            def sums_to_all(h):
                if h >= 2:
                    pe.wait_ge(seg_ready, h - 1)
                mm(ps[:, h % 2, 0:T], hb[:, h, :], acT[:], start=True, stop=True).then_inc(bc_full, 1)

            def y_diag(h):
                c, a = divmod(h, 2)
                pe.wait_ge(sco_ready, h + 1)
                if c >= 2:
                    pe.wait_ge(yd_out, c - 1)
                for t in range(NT + 1):
                    w = P if t < NT else TS
                    i = mm(ps[a * PD:(a + 1) * PD, 2 + c % 2, t * P:t * P + w], xdt_tok[0:w, t, h * PD:(h + 1) * PD],
                           sco[0:w, h % 2, t * P:t * P + w], start=True, stop=True)
                i.then_inc(yd_full, 1)

            sums_to_all(0)
            for h in range(HS):
                if h + 1 < HS:
                    sums_to_all(h + 1)
                y_diag(h)

            for c in range(SC):
                i = mm(ps[:, 4 + c // 4, (c % 4) * P:(c % 4 + 1) * P], h1T[:, c * P:(c + 1) * P],
                       xc[:, SC + G + c // GCH, P:2 * P], start=True, stop=True)
            i.then_inc(yo_full, 1)
            for c in range(SC):
                o = ps[:, 6 + c // 4, (c % 4) * P:(c % 4 + 1) * P]
                mm(o, xde[:, 1, c * P:(c + 1) * P], B_tok[:, 0, c // GCH, :], start=True, stop=False)
                i = mm(o, xde[:, 2, c * P:(c + 1) * P], B_tok[:, 1, c // GCH, :], start=False, stop=True)
            i.then_inc(ssm_full, 1)
            pe.wait_ge(yd_out, SC)
            pe.wait_ge(ssm_out, 1)
            pe.wait_ge(yo_out, 1)
            for b in range(NB):
                pe.wait_ge(h0_full[b % 2], 16 * (b // 2 + 1))
                if b:
                    pe.wait_ge(h0T_out, b)
                for c in range(SC):
                    i = tr(ps[:, c // 4, (c % 4) * P:(c % 4 + 1) * P], h0[:, b % 2, c, :], P)
                i.then_inc(h0T_full, 1)
                pe.wait_ge(bm_ready, b + 1)
                if b:
                    pe.wait_ge(hn_out, b)
                for c in range(SC):
                    i = mm(ps[:, 2 + c // 4, (c % 4) * P:(c % 4 + 1) * P], xde_s[:, c * P:(c + 1) * P],
                           bm_s[:, c // GCH, :], start=True, stop=True)
                i.then_inc(hn_full, 1)
                pe.wait_ge(h0T_out, b + 1)
                for c in range(SC):
                    i = mm(ps[:, 4, (c * NB + b) * LS:(c * NB + b + 1) * LS], h0T[:, c, :],
                           xc[:, SC + G + c // GCH, SEQ + b * LS:SEQ + (b + 1) * LS], start=True, stop=True)
                i.then_inc(ys_full, 1)
            pe.wait_ge(ysq_ready, 1)
            for g in range(G):
                sums(sq1, range(g * GCH, (g + 1) * GCH), 6 + g)

            pe.wait_ge(y_lo, 1)
            pe.wait_ge(ov_lo, 1)
            yx = (lambda k: yhi[:, k, :] if k < SC else ohi[:, k - SC, :]), \
                 (lambda k: ylo[:, k, :] if k < SC else olo[:, k - SC, :])
            pairs(2, 4, *yx)
            adaq(4)
            pe.wait_ge(group_free, 2 + ZX_GROUPS + QKV_GROUPS + 4)
            norm_sums(sq2)
            norm_sums(sq2)

            pe.wait_ge(h_lo, 2)

            def up(r, s):
                out0 = r if isinstance(r, int) else 2
                if out0 >= 2:
                    pe.wait_ge(f_add, 4 * r - 5 + s)
                elif r == 1:
                    pe.wait_ge(f_u, s + 1)
                for j in range(RING):
                    pe.wait_ge(lo_ready, 4 * pos.split + j + 1)
                    unit3(j, 4 * s, lambda q: (h2hi[:, j * QC + q, :], h2lo[:, j * QC + q, :]), j == 0, j == RING - 1)\
                        .then_inc(w_used, 1)
                pos.step(quad=1, split=1)

            def down(r, last=False):
                pe.wait_ge(f_lo, r + 1)
                for n in range(4):
                    if n < 2:
                        if last:
                            pe.wait_ge(f_add, 4 * r - 1 + n)
                        else:
                            pe.wait_ge(f_u, 2 * r + 3 + n)
                    else:
                        pe.wait_ge(f_add, 4 * r + n - 1)
                    pe.wait_ge(lo_ready, 4 * pos.split + n + 1)
                    unit3(n, 4 * (n % 2), lambda q: (ghi[:, q, :], glo[:, q, :]), True, True).then_inc(w_used, 1)
                pos.step(quad=1, split=1)

            ROUNDS = FC // MC
            up(0, 0)
            up(0, 1)
            up(1, 0)
            up(1, 1)
            down(0)
            with pe.Fori(2, ROUNDS) as r:
                pos.enter(r, 2, quad=3, split=3)
                up(r, 0)
                up(r, 1)
                down(r - 1)
                pos.leave(ROUNDS - 2)
            down(ROUNDS - 1, last=True)

            norm_sums(sq3)
            pe.wait_ge(f_col, 2 * ROUNDS)
            pe.wait_ge(fcomp_ready, 1)
            for n in range(11):
                i = tr(ps[:, 5 + n // 4, (n % 4) * P:(n % 4 + 1) * P], fcomp[:, n, :], P)
            i.then_inc(fc_T, 1)
            for r in range(2):
                i = tr(ps[0:2 * FC, 4, r * P:(r + 1) * P], pcol[:, :, r], P)
            i.then_inc(fc_T, 1)
            pe.wait_ge(fc_o, 2)
            pe.wait_ge(x2_ready, 2)
            for n in range(4 * (NT + 1)):
                t, g = divmod(n, 4)
                w = P if t < NT else TS
                if n >= 8:
                    pe.wait_ge(ys_o, n - 7)
                for m in range(4):
                    i = tr(ps[0:w, n % 8, m * P:(m + 1) * P], xT[:, 4 * g + m, t * P:t * P + w], P)
                i.then_inc(ys_T, 1)

        @block.scalar
        def _(act):
            pos = Place()
            c = Count(act, act_c)
            fn = act.activation

            for r0, src in ((0, c_prompt), (1, c_sample)):
                act.dma_start(crow[r0:r0 + src.shape[0]], src).then_inc(in_c, 16)
            for n, r0, src in ((0, 0, b_ada), (0, MODC, g_pre_mix), (0, MODC + KC, g_post_mix), (1, 0, g_pre_ffn),
                               (1, KC, g_post_ffn), (1, V_CB, conv_b), (1, V_GS, g_ssd_norm), (2, 0, ffn_conv_b)):
                k = src.shape[1] // P
                act.dma_start(vrow[r0:r0 + k, n, :], src[0].rearrange("(c p) -> c p", p=P)).then_inc(in_vec, 16)
            act.dma_start(vrow[V_CW:V_CB, 1, :], conv_w[0].rearrange("k (c p) -> (k c) p", p=P)).then_inc(in_vec, 16)
            act.dma_start(vrow[0:2 * FC, 3:6, :], ffn_conv_w[0].rearrange("k (c p) -> c k p", p=P)).then_inc(in_vec, 16)
            for t in range(NT):
                act.dma_start(xrow[:, t, :], x_prompt[0, t * P:(t + 1) * P]).then_inc(in_x, 16)
            act.dma_start(xrow[0:TS, NT, :], x_sample.rearrange("b t d -> (b t) d")).then_inc(in_x, 16)
            act.dma_start(frow[:].rearrange("p c f -> p (c f)"),
                          state_ffn_conv[0].rearrange("b r (g x) -> (b r g) x", g=8)).then_inc(in_ctx, 16)
            act.dma_start(srow[0:96].rearrange("p c f -> p (c f)"),
                          state_conv[0].rearrange("b r (g x) -> (b r g) x", g=4)).then_inc(in_ctx, 16)
            for dst, src in ((dtb, dt_bias), (nega, a_log), (dskip, d_skip)):
                act.dma_start(dst[:], src.rearrange("o h -> h o")).then_inc(in_misc, 16)
            act.dma_start(sbb[:], sb_bias.to_broadcast([P, HA])).then_inc(in_misc, 16)
            act.dma_start(wdt[:], w_in_v[:, COL_DT:COL_Q].rearrange("(k p) n -> p k n", p=P)).then_inc(in_misc, 16)
            act.dma_start(ptab[:], page_table.rearrange("b n -> (b n)").unsqueeze(0)).then_inc(in_pt, 16)

            act.wait_ge(rows_T, 4)
            fn(cT[:].rearrange("p k s -> p (k s)"), ps[:, 1, 256:256 + KC * NSEQ], ACT.Silu).then_inc(c_ready, 1)
            for n in range(12):
                t, g = divmod(n, 4)
                w = P if t < NT else TS
                act.wait_ge(x_T, n + 1)
                fn(xT[:, 4 * g:4 * g + 4, t * P:t * P + w],
                   ps[:, (6 + n) % 8, 0:4 * w].rearrange("p (m w) -> p m w", m=4), ACT.Copy).then_inc(x_out, 1)
            act.wait_ge(x_out, 12)
            act.sem_inc(group_free, 2)
            norms = [0]

            def square(dst, src):
                fn(dst[:], src[:], ACT.Square).then_inc(sq_ready, 1)

            def root(bank, dst, width):
                norms[0] += 1
                act.wait_ge(sum_ready, norms[0])
                fn(dst, ps[:, bank, 0:T], ACT.Sqrt, scale=1.0 / width, bias=eps[:]).then_inc(root_ready, 1)

            modulated = [0]

            def modulate(f, hi, shift):
                modulated[0] += 1
                act.wait_ge(xr_ready, modulated[0])
                for k in range(KC):
                    i = fn(f[:, k, 0:SEQ], f[:, k, 0:SEQ], ACT.Identity, scale=gainT[:, k, 0:1], bias=modT[:, shift + k, 0:1])
                i.then_inc(hp_ready, 1)
                act.wait_ge(hp_ready, modulated[0])
                act.wait_ge(hs_ready, modulated[0])
                fn(hi[:], f[:], ACT.Copy).then_inc(h_hi, 1)

            square(sq0, xT)
            act.wait_ge(consts, 2)
            root(2, rT[:], DM)
            modulate(hf, hhi, SH1)
            act.wait_ge(dt_full, 1)
            fn(dtraw[:], ps[0:HS, 7, 0:T], ACT.Copy).then_inc(dt_out, 1)

            def hi(j):
                act.wait_ge(raw_full[j], 16 * (pos.quad + 1))
                if not (isinstance(pos.split, int) and 4 * pos.split + j < 2):
                    act.wait_ge(w_used, 4 * pos.split + j - 1)
                fn(whi[:, j % 2], raw[:, j], ACT.Copy).then_inc(hi_ready, 1)

            def group(out, chunk):
                for j in range(RING):
                    hi(j)
                pos.step(quad=1, split=1)
                act.wait_ge(w_used, 4 * pos.split)
                b = 4 * side[0]
                fn(out[:, ds(chunk, MC), :], ps[:, b:b + 4, 0:T], ACT.Copy).then_inc(group_free, 1)
                side[0] ^= 1
                pos.step(quad=1)

            side = [0]
            pos.step(quad=8)
            group(proj, 0)
            with act.Fori(0, 2) as i:
                pos.enter(i, 0, quad=4, split=2)
                group(proj, i * (2 * MC) + MC)
                group(proj, i * (2 * MC) + 2 * MC)
                pos.leave(2)
            with act.Fori(0, 3) as i:
                pos.enter(i, 0, quad=4, split=2)
                group(proj, i * (2 * MC) + QP)
                group(proj, i * (2 * MC) + QP + MC)
                pos.leave(3)

            for t in range(NT + 1):
                w = P if t < NT else TS
                act.wait_ge(tok_full, t + 1)
                if t:
                    act.wait_ge(tok_dma, 16 * t)
                fn(kstage[0:w].rearrange("p (b x) -> p b x", b=2), ps[0:w, 2 * (t % 2):2 * (t % 2) + 2, :], ACT.Copy)\
                    .then_inc(ktok_out, 1)
            act.wait_ge(ccol_T, 1)
            fn(cout[:], ps[0:108, 7, 0:3 * P].rearrange("p (c f) -> p c f", c=3), ACT.Copy).then_inc(ccol_out, 1)

            n_z = [0]

            def soft(x):
                n_z[0] += 1
                act.wait_ge(z_na, n_z[0])
                c.link(fn(x, x, ACT.Exp))
                fn(x, x, ACT.Ln, bias=1.0).then_inc(z_e, 1)

            soft(pa[0:TS, 0:HA * TS])
            act.wait_ge(w_d, 1)
            fn(pa[0:TS, 0:HA * TS], pz[0:TS, 0:HA * TS], ACT.Exp).then_inc(w_e, 1)
            for h in range(HA):
                soft(pa[:])
                act.wait_ge(w_d, h + 2)
                fn(pw[:], pz[:], ACT.Exp).then_inc(w_e, 1)

            def k_half(p, n):
                act.wait_ge(kT_full, n + 1)
                if not (isinstance(n, int) and n < 2):
                    act.wait_ge(page_scored, n - 1)
                fn(kt[:, p % 2, 0:4, :], ps[:, 2 * (p % 2), :].rearrange("p (h x) -> p h x", h=4), ACT.Copy)\
                    .then_inc(kT_act, 1)

            def weights(b):
                act.wait_ge(dn_d, b + 1)
                if not (isinstance(b, int) and b == 0):
                    act.wait_ge(page_summed, b * NPG)
                fn(dw[:], dz[:], ACT.Exp).then_inc(dn_w, 1)

            def sequence(b):
                for p in range(NPG):
                    k_half(p, b * NPG + p)
                    if p == 1 and not (isinstance(b, int) and b == 0):
                        weights(b - 1)
                act.wait_ge(dn_na, b + 1)
                c.link(fn(da[:], da[:], ACT.Exp))
                fn(da[:], da[:], ACT.Ln, bias=1.0).then_inc(dn_e, 1)

            sequence(0)
            sequence(1)
            with act.Fori(2, NB) as b:
                c.enter(b, 2, 1)
                sequence(b)
                c.leave(NB - 2)
            weights(NB - 1)

            act.wait_ge(do_out, NB)
            fn(ohi[:], oT[:], ACT.Copy).then_inc(ov_hi, 1)
            fn(proj[:, ZP:ZP + SC, :], proj[:, ZP:ZP + SC, :], ACT.Silu).then_inc(z_silu, 1)
            act.wait_ge(conv_done, 1)
            fn(xc[:], xc[:], ACT.Silu).then_inc(silu_done, 1)
            act.wait_ge(in_misc, 16 * 5)
            fn(nega[:], nega[:], ACT.Exp).then_inc(a_ready, 1)
            act.wait_ge(dt_na, 1)
            fn(t2[:], t2[:], ACT.Exp).then_inc(dt_e, 1)
            act.wait_ge(dt_e, 1)
            fn(dtT[:], t2[:], ACT.Ln, bias=1.0).then_inc(dt_ln, 1)
            act.wait_ge(ac_full, 1)
            for t in range(4):
                w = P if t < 3 else TS
                i = fn(dend_tok[0:w, t, :], ps[0:w, 3, t * HS:(t + 1) * HS], ACT.Exp)
            i.then_inc(ac_exp, 1)
            for k in range(SC):
                act.wait_ge(acE_full, k + 1)
                fn(eaE[:, k, :], ps[:, 6 + k % 2, 0:P + TS], ACT.Exp).then_inc(eaE_made, 1)
            act.wait_ge(B_full, 1)
            fn(B_tok[:, 0:2], ps[:, 4, :].rearrange("p (t g n) -> p t g n", t=2, g=G), ACT.Copy)
            fn(B_tok[0:TS, 2], ps[0:TS, 5, 0:G * NS].rearrange("p (g n) -> p g n", g=G), ACT.Copy).then_inc(B_out, 1)
            act.wait_ge(h1_full, 1)
            fn(h1T[:].rearrange("p (g x) -> p g x", g=G), ps[:, 0:2, :], ACT.Copy).then_inc(h1_out, 1)
            for h in range(HS):
                act.wait_ge(seg_ready, h + 1)
                if h >= 2:
                    act.wait_ge(sco_ready, h - 1)
                fn(dec[:, h % 2], seg[:, h % 2], ACT.Exp).then_inc(dec_ready, 1)
            for b in range(NB):
                act.wait_ge(h0T_full, b + 1)
                if b:
                    act.wait_ge(ys_full, b)
                fn(h0T[:].rearrange("p (b c) x -> p b (c x)", b=2), ps[:, 0:2, :], ACT.Copy).then_inc(h0T_out, 1)
            act.wait_ge(y_gated, 1)
            fn(sq1[:], yT[:], ACT.Square).then_inc(ysq_ready, 1)
            for g in range(G):
                root(6 + g, rg[:, g], GCH * P)
            act.wait_ge(y_normed, 1)
            for k in range(SC):
                i = fn(yhi[:, k, :], yT[:, k, :], ACT.Copy, scale=vecT[:, 1, V_GS + k:V_GS + k + 1])
            i.then_inc(y_hi, 1)

            side[0] = 1
            for half in range(2):
                act.wait_ge(hn_dma[half], 16 * (NB // 2))
            with act.Fori(0, 2) as i:
                pos.enter(i, 0, quad=4, split=2)
                group(mT, i * (2 * MC))
                group(mT, i * (2 * MC) + MC)
                pos.leave(2)
            pos.step(quad=1)
            act.wait_ge(group_free, 2 + ZX_GROUPS + QKV_GROUPS + 4)
            square(sq2, mT)
            root(2, rT[:], DM)
            act.wait_ge(x2_ready, 1)
            square(sq2, xT)
            root(2, rT[:], DM)
            modulate(h2f, h2hi, SH2)

            def high_g(r):
                act.wait_ge(f_gt, r + 1)
                if not (isinstance(r, int) and r == 0):
                    act.wait_ge(w_used, split_g[0])
                fn(ghi[:], gt[:], ACT.Copy).then_inc(f_hi, 1)

            split_g = [0]

            def out_of_psum(r, s):
                u = (ug, uv)[s]
                if not (isinstance(r, int) and r == 0):
                    act.wait_ge(f_c, 2 * (r - 1) + s + 1)
                    act.wait_ge(f_col, 2 * (r - 1) + s + 1)
                fn(u[:, :, 2:2 + SEQ], ps[:, 4 * s:4 * s + 4, 0:SEQ], ACT.Copy)
                fn(u[:, :, SEQ + 2:UP].rearrange("p m (b t) -> p m b t", b=NB)[:, :, :, 2:2 + LS],
                   ps[:, 4 * s:4 * s + 4, SEQ:T].rearrange("p m (b t) -> p m b t", b=NB), ACT.Copy).then_inc(f_u, 1)

            def silu(r):
                act.wait_ge(f_c, 2 * r + 1)
                fn(cg[:, :, 0:UP - 2], cg[:, :, 0:UP - 2], ACT.Silu).then_inc(f_s, 1)

            def round_(r, out):
                for s in range(2):
                    hi(0)
                    hi(1)
                    if s == 0 and out:
                        split_g[0] = 4 * pos.split
                        high_g(r - 1)
                    if s == 1:
                        act.wait_ge(w_used, 4 * pos.split)
                        out_of_psum(r, 0)
                    hi(2)
                    hi(3)
                    pos.step(quad=1, split=1)
                if out:
                    hi(0)
                    hi(1)
                act.wait_ge(w_used, 4 * pos.split)
                out_of_psum(r, 1)
                silu(r)
                if out:
                    hi(2)
                    hi(3)
                    pos.step(quad=1, split=1)

            ROUNDS = FC // MC
            round_(0, False)
            round_(1, True)
            with act.Fori(2, ROUNDS) as r:
                pos.enter(r, 2, quad=3, split=3)
                round_(r, True)
                pos.leave(ROUNDS - 2)
            split_g[0] = 4 * pos.split
            high_g(ROUNDS - 1)
            for j in range(RING):
                hi(j)
            pos.step(quad=1, split=1)
            act.wait_ge(f_add, 4 * ROUNDS)
            square(sq3, fT)
            root(2, rT[:], DM)
            act.wait_ge(fc_T, 2)
            fn(fstage[:, 0:8].rearrange("p (b c) f -> p b (c f)", b=2), ps[:, 5:7, :], ACT.Copy)
            fn(fstage[:, 8:11].rearrange("p c f -> p (c f)"), ps[:, 7, 0:3 * P], ACT.Copy).then_inc(fc_o, 1)
            fn(fpstage[:].rearrange("p r f -> p (r f)"), ps[0:2 * FC, 4, 0:2 * P], ACT.Copy).then_inc(fc_o, 1)

        @block.vector
        def _(dve):
            pos = Place()
            c = Count(dve, dve_c)
            tt, ts, stt, cp = dve.tensor_tensor, dve.tensor_scalar, dve.scalar_tensor_tensor, dve.tensor_copy
            MUL, ADD, SUB, MIN, MAX = ALU.mult, ALU.add, ALU.subtract, ALU.min, ALU.max

            dve.wait_ge(consts, 2)
            dve.wait_ge(rows_T, 4)
            for n, k in ((0, P), (1, V_GS + SC)):
                cp(vecT[:, n, 0:k], ps[:, 0, n * P:n * P + k])
            cp(vecT[:, 2:4, 0:2 * FC], ps[:, 0, 2 * P:4 * P].rearrange("p (v k) -> p v k", v=2)[:, :, 0:2 * FC])
            dve.wait_ge(c_ready, 1)
            c.mark(cp(vecT[:, 4:6, 0:2 * FC], ps[:, 1, 0:2 * P].rearrange("p (v k) -> p v k", v=2)[:, :, 0:2 * FC]))
            rows = ctxT[:].rearrange("p (g c) r -> p c r g", c=11)
            for n in range(3):
                k = min(4, 11 - 4 * n)
                cp(rows[:, 4 * n:4 * n + k], ps[:, 2 + n, 0:k * P].rearrange("p (c r g) -> p c r g", c=k, g=8))
            for g in range(4):
                i = cp(xpad[:, 3 * g:3 * g + 3, :, 0:KCONV - 1],
                       ps[:, 5, 0:288].rearrange("p (c b k g) -> p g c b k", c=3, b=NB, g=4)[:, g])
            i.then_inc(rows_out, 1)
            dve.wait_ge(in_misc, 16 * 5)
            c.mark(cp(zbias[:], sbb[:].unsqueeze(1).unsqueeze(3).to_broadcast([P, NPG, HA, LS])))

            def ada_out(bank):
                dve.wait_ge(ada_used, 4 * (pos.ada + 1))
                tt(modT[:, ds(pos.ada * MC, MC), :], ps[:, bank, 0:MC * NSEQ].rearrange("p (m s) -> p m s", m=MC),
                   vecT[:, 0, ds(pos.ada * MC, MC)].unsqueeze(2).to_broadcast([P, MC, NSEQ]), ADD).then_inc(ada_free, 1)
                pos.step(quad=1, ada=1)

            c.settle()
            norms = [0]

            def normed(dst, src, r, chunks):
                norms[0] += 1
                dve.wait_ge(root_ready, norms[0])
                c.link(dve.reciprocal(r, r))
                return tt(dst, src, r.unsqueeze(1).to_broadcast([P, chunks, T]), MUL)

            def gain(scale, g, plus):
                vec = vecT[:, g[0], g[1]:g[1] + KC].unsqueeze(2).to_broadcast([P, KC, NSEQ])
                return stt(gainT[:], modT[:, scale:scale + KC, :], plus, vec, ADD, MUL)

            def per_seq(m):
                return m[:, :, 1:NSEQ].unsqueeze(3).to_broadcast([P, KC, NB, LS])

            ada_out(4)
            with dve.Fori(1, 8) as i:
                pos.enter(i, 1, quad=1, ada=1)
                ada_out(4)
                pos.leave(7)
            dve.wait_ge(ada_free, 8)

            def prepare(f, src, scale, shift, g, n):
                c.mark(gain(scale, g, 1.0))
                normed(f[:], src[:], rT[:], KC).then_inc(xr_ready, 1)
                dve.wait_ge(xr_ready, n)
                c.link(tt(smp(f), smp(f), per_seq(gainT), MUL))
                tt(smp(f), smp(f), per_seq(modT[:, shift:shift + KC, :]), ADD).then_inc(hs_ready, 1)

            def low(lo_, f, hi_, n):
                dve.wait_ge(h_hi, n)
                tt(lo_[:], f[:], hi_[:].bitcast(F32), SUB).then_inc(h_lo, 1)

            prepare(hf, xT, SC1, SH1, V_PRE_MIX, 1)
            low(hlo, hf, hhi, 1)

            def lo(j):
                dve.wait_ge(hi_ready, 4 * pos.split + j + 1)
                tt(wlo[:, j % 2], raw[:, j], whi[:, j % 2].bitcast(F32), SUB).then_inc(lo_ready, 1)

            def pair(bank0):
                for j in range(RING):
                    lo(j)
                pos.step(quad=1, split=1)
                ada_out(4 - bank0)

            def pairs(turns, bank0):
                with dve.Fori(0, turns) as i:
                    pos.enter(i, 0, quad=4, split=2, ada=2)
                    pair(bank0)
                    pair(4 - bank0)
                    pos.leave(turns)

            pair(0)
            pairs(2, 4)
            pairs(3, 4)

            dve.wait_ge(group_free, 2 + ZX_GROUPS + QKV_GROUPS)
            for g in range(4):
                chunks = slice(XP + 3 * g, XP + 3 * g + 3)
                cp(ccol[:, :, 0:3, g], proj[:, chunks, SEQ - 3:SEQ])
                i = cp(ccol[:, :, 3:27, g].rearrange("p c (b k) -> p c b k", b=NB), smp(proj)[:, chunks, :, LS - 3:LS])
            i.then_inc(ccol_ready, 1)
            c.mark(cp(xpad[:, :, :, KCONV - 1:], smp(proj)[:, XP:XP + XC]))
            for t in range(NT + 1):
                w = P if t < NT else TS
                n = 3 + t
                dve.wait_ge(tok_full, n + 1)
                cp(vtok[0:w, t, :].rearrange("p (b x) -> p b x", b=2), ps[0:w, 2 * (n % 2):2 * (n % 2) + 2, :])\
                    .then_inc(vtok_out, 1)

            nh = [0]

            def softplus(z, a, sp, spm, mask):
                nh[0] += 1
                dve.wait_ge(z_e, nh[0])
                c.link(stt(sp, z, 0.0, a, MAX, ADD))
                tt(spm, sp, mask, MUL).then_inc(z_sp, 1)
                c.link(tt(z, z, sp, SUB))
                dve.wait_ge(tail_full, nh[0])

            HT = HA * TS
            dve.wait_ge(z_full, 1)
            c.link(ts(pz[0:TS, 0:HT], ps[0:TS, 4, 0:HT], SCALE, None, MUL))
            h_t = lambda a: a[0:TS, 0:HT].rearrange("p (h t) -> p h t", h=HA)
            c.link(tt(h_t(pz), h_t(pz), sbb[0:TS].unsqueeze(2).to_broadcast([TS, HA, TS]), ADD))
            stt(pa[0:TS, 0:HT], pz[0:TS, 0:HT], -1.0, pz[0:TS, 0:HT], MUL, MIN).then_inc(z_na, 1)
            mask_s = before_s[:].unsqueeze(1).to_broadcast([TS, HA, TS])
            nh[0] += 1
            dve.wait_ge(z_e, 1)
            c.link(stt(psp[0:TS, 0:HT], pz[0:TS, 0:HT], 0.0, pa[0:TS, 0:HT], MAX, ADD))
            tt(sp_new[:], h_t(psp), mask_s, MUL).then_inc(z_sp, 1)
            c.link(tt(pz[0:TS, 0:HT], pz[0:TS, 0:HT], psp[0:TS, 0:HT], SUB))
            dve.wait_ge(tail_full, 1)
            tt(pz[0:TS, 0:HT], pz[0:TS, 0:HT], ps[0:TS, 5, 0:HT], SUB).then_inc(w_d, 1)
            dve.wait_ge(w_e, 1)
            tt(h_t(pa), h_t(pa), mask_s, MUL).then_inc(w_ready, 1)
            dve.wait_ge(o_full, 1)
            cp(o_new[:].rearrange("p h t -> p (h t)"), ps[:, 6, 0:HT]).then_inc(o_out, 1)
            for h in range(HA):
                dve.wait_ge(z_full, h + 2)
                c.link(ts(pz[:], ps[:, h % 2, 0:3 * P], SCALE, sbb[:, h:h + 1], MUL, ADD))
                stt(pa[:], pz[:], -1.0, pz[:], MUL, MIN).then_inc(z_na, 1)
                softplus(pz[:], pa[:], psp[:], pspm[:], cmask[:])
                tt(pz[:], pz[:], ps[:, 2 + h % 2, 0:3 * P], SUB).then_inc(w_d, 1)
                dve.wait_ge(w_e, h + 2)
                tt(pw[:], pw[:], cmask[:], MUL).then_inc(w_ready, 1)
                dve.wait_ge(o_full, h + 2)
                cp(oT[:, h, 0:SEQ], ps[:, 4 + h % 2, 0:SEQ]).then_inc(o_out, 1)

            def k_half(p, n):
                dve.wait_ge(kT_full, n + 1)
                if not (isinstance(n, int) and n < 2):
                    dve.wait_ge(page_scored, n - 1)
                cp(kt[:, p % 2, 4:8, :], ps[:, 2 * (p % 2) + 1, :].rearrange("p (h x) -> p h x", h=4)).then_inc(kT_dve, 1)

            flat = lambda a: a[:].rearrange("p g h t -> p (g h t)")

            def log_weights(b):
                dve.wait_ge(dtail_full, b + 1)
                tt(flat(dz), flat(dz), ps[:, 6, 0:NPG * HQ], SUB).then_inc(dn_d, 1)

            def summed(b):
                dve.wait_ge(page_summed, NPG * (b + 1))
                tt(oT[:, :, ds(b * LS + SEQ, LS)], ps[:, 5, 0:HQ].rearrange("p (h t) -> p h t", h=HA),
                   o_new[:, :, ds(b * LS, LS)], ADD).then_inc(do_out, 1)

            def sequence(b):
                first = isinstance(b, int) and b == 0
                for p in range(NPG):
                    k_half(p, b * NPG + p)
                    if p == 1 and not first:
                        log_weights(b - 1)
                if not first:
                    summed(b - 1)
                    dve.wait_ge(dn_w, b)
                dve.wait_ge(page_scored, NPG * (b + 1))
                c.link(stt(flat(dz), ps[:, 4, 0:NPG * HQ], SCALE, flat(zbias), MUL, ADD))
                stt(flat(da), flat(dz), -1.0, flat(dz), MUL, MIN).then_inc(dn_na, 1)
                dve.wait_ge(dn_e, b + 1)
                stt(flat(dsp), flat(dz), 0.0, flat(da), MAX, ADD).then_inc(dn_sp, 1)
                dve.wait_ge(dn_sp, b + 1)
                c.link(tt(flat(dz), flat(dz), flat(dsp), SUB))

            dve.wait_ge(ccol_dma, 32)
            sequence(0)
            sequence(1)
            with dve.Fori(2, NB) as b:
                c.enter(b, 2, 2)
                sequence(b)
                c.leave(NB - 2)
            log_weights(NB - 1)
            summed(NB - 1)
            dve.wait_ge(ov_hi, 1)
            tt(olo[:], oT[:], ohi[:].bitcast(F32), SUB).then_inc(ov_lo, 1)

            dve.wait_ge(tok_dma, 16 * 6)
            cw = lambda k, x: vecT[:, 1, V_CW + k * XC + x:V_CW + k * XC + x + 1]
            for x in range(XC):
                i = ts(xc[:, x, 0:SEQ], proj[:, XP + x, 0:SEQ], cw(KCONV - 1, x), vecT[:, 1, V_CB + x:V_CB + x + 1], MUL, ADD)
            c.link(i)
            for d in range(1, KCONV):
                for x in range(XC):
                    i = stt(xc[:, x, d:SEQ], proj[:, XP + x, 0:SEQ - d], cw(KCONV - 1 - d, x), xc[:, x, d:SEQ], MUL, ADD)
                c.link(i)
            taps = [vecT[:, 1, v:v + XC].unsqueeze(2).unsqueeze(3).to_broadcast([P, XC, NB, LS])
                    for v in [V_CW + k * XC for k in range(KCONV)] + [V_CB]]
            c.link(tt(smp(xc), xpad[:, :, :, 0:LS], taps[0], MUL))
            c.link(tt(smp(xc), smp(xc), taps[KCONV], ADD))
            tmp = ctmp[:].rearrange("p n (b t) -> p n b t", b=NB)
            for k in range(1, KCONV):
                c.link(tt(tmp, xpad[:, :, :, k:k + LS], taps[k], MUL))
                i = tt(smp(xc), smp(xc), tmp, ADD)
                if k < KCONV - 1:
                    c.link(i)
            i.then_inc(conv_done, 1)

            c.link(ts(t1[:], dtraw[:], dtb[:], None, ADD))
            stt(t2[:], t1[:], -1.0, t1[:], MUL, MIN).then_inc(dt_na, 1)
            dve.wait_ge(a_ready, 1)
            c.link(ts(nega[:], nega[:], -1.0, None, MUL))
            dve.wait_ge(dt_ln, 1)
            c.link(ts(acT[:], t2[:], 1.0, None, ADD))
            c.link(ts(acT[:], acT[:], 1.0, None, SUB))
            c.link(ts(dA_T[:], acT[:], 0.0, None, ALU.is_equal))
            c.mark(tt(acT[:], acT[:], dA_T[:], ADD))
            c.link(tt(dtT[:], dtT[:], dA_T[:], ADD))
            c.mark(dve.reciprocal(acT[:], acT[:]))
            c.link(tt(dtT[:], dtT[:], t2[:], MUL))
            c.link(tt(dtT[:], dtT[:], acT[:], MUL))
            c.link(stt(dtT[:], t1[:], 0.0, dtT[:], MAX, ADD))
            ts(dA_T[:], dtT[:], nega[:], None, MUL).then_inc(dt_done, 1)
            dve.wait_ge(dA_full, 1)
            cp(dA_tok[:, 0:NT, :].rearrange("p t h -> p (t h)"), ps[:, 0, 0:NT * HS])
            cp(dA_tok[0:TS, NT, :], ps[0:TS, 0, NT * HS:(NT + 1) * HS]).then_inc(dA_ready, 1)
            dve.wait_ge(ac_full, 1)
            cp(ac_tok[:, 0:NT, :].rearrange("p t h -> p (t h)"), ps[:, 1, 0:NT * HS])
            cp(ac_tok[0:TS, NT, :], ps[0:TS, 1, NT * HS:(NT + 1) * HS])
            cp(acT[:], ps[0:HS, 2, 0:T])
            cp(dskE[:], ps[:, 4, 0:SC]).then_inc(ac_out, 1)
            dve.wait_ge(silu_done, 1)
            for k in range(SC):
                dve.wait_ge(dtE_full, k + 1)
                tt(xdtT[:, k, :], xc[:, k, :], ps[:, 4 + k % 2, 0:T], MUL).then_inc(xdt_made, 1)
            for t in range(NT + 1):
                w = P if t < NT else TS
                dve.wait_ge(xdt_full, t + 1)
                cp(xdt_tok[0:w, t, :].rearrange("p (b x) -> p b x", b=2), ps[0:w, 2 * (t % 2):2 * (t % 2) + 2, :])\
                    .then_inc(xdt_out, 1)
            dve.wait_ge(hb_ready, 1)
            dve.wait_ge(cb_full, 1)
            for g in range(G):
                tt(cbm[:, g, 0:SEQ].rearrange("p (t l) -> p t l", t=NT), ps[:, 6 + g, 0:SEQ].rearrange("p (t l) -> p t l", t=NT),
                   incl[:].unsqueeze(1).to_broadcast([P, NT, P]), MUL)
                i = tt(cbm[0:TS, g, SEQ:T], ps[0:TS, 6 + g, SEQ:T], incl_s[:], MUL)
            i.then_inc(cbm_made, 1)
            dve.wait_ge(ac_exp, 1)
            dve.wait_ge(xdt_out, 3)
            heads = lambda a: a.rearrange("p (h d) -> p h d", d=PD)
            for n, t in ((0, 0), (1, 0), (2, 1)):
                tt(heads(xde[:, n]), heads(xdt_tok[:, t]), dend_tok[:, n, :].unsqueeze(2).to_broadcast([P, HS, PD]), MUL)
            tt(heads(xde_s[:]), heads(xdt_tok[0:TS, NT]), dend_tok[0:TS, 3, :].unsqueeze(2).to_broadcast([TS, HS, PD]), MUL)\
                .then_inc(xde_made, 1)

            def decays(h):
                dve.wait_ge(bc_full, h + 1)
                for t in range(NT + 1):
                    w = P if t < NT else TS
                    i = ts(seg[:, h % 2, t * P:t * P + w], ps[:, h % 2, t * P:t * P + w], ac_tok[:, t, h:h + 1], 0.0, SUB, MIN)
                i.then_inc(seg_ready, 1)

            def weigh(h):
                dve.wait_ge(dec_ready, h + 1)
                if h >= 2:
                    dve.wait_ge(yd_full, h - 1)
                tt(sco[:, h % 2], dec[:, h % 2], cbm[:, h // (HS // G)], MUL).then_inc(sco_ready, 1)

            def diag_out(k):
                dve.wait_ge(yd_full, 2 * k + 2)
                stt(yT[:, k, :], xc[:, k, :], dskE[:, k:k + 1], ps[:, 2 + k % 2, 0:T], MUL, ADD).then_inc(yd_out, 1)

            dve.wait_ge(cbm_made, 1)
            decays(0)
            for h in range(HS):
                if h + 1 < HS:
                    decays(h + 1)
                weigh(h)
                if h % 2 and h > 1:
                    diag_out(h // 2 - 1)
            diag_out(SC - 1)
            dve.wait_ge(yd_out, SC)
            dve.wait_ge(yo_full, 1)
            dve.wait_ge(eaE_made, SC)
            c.link(tt(ytmp[:], eaE[:, :, 0:P], ps[:, 4:6, :].rearrange("p b (c x) -> p (b c) x", c=4), MUL))
            tt(yT[:, :, P:2 * P], yT[:, :, P:2 * P], ytmp[:], ADD).then_inc(yo_out, 1)
            dve.wait_ge(ssm_full, 1)
            cp(hnew[:, 1].rearrange("p (b c) n -> p b (c n)", b=2), ps[:, 6:8, :]).then_inc(ssm_out, 1)
            for b in range(NB):
                if b:
                    dve.wait_ge(hn_full, b)
                ts(bm_s[:].rearrange("p g n -> p (g n)"), B_tok[0:TS, NT].rearrange("p g n -> p (g n)"),
                   seq_of[:, b:b + 1], None, MUL).then_inc(bm_ready, 1)
                dve.wait_ge(hn_full, b + 1)
                if b == 1:
                    dve.wait_ge(ssm_dma, 16)
                if b >= 2:
                    dve.wait_ge(hn_dma[b % 2], 16 * (b // 2))
                for k in range(SC):
                    last_token = P + b * LS + LS - 1
                    i = stt(hnew[:, b % 2, k, :], h0[:, b % 2, k, :], eaE[:, k, last_token:last_token + 1],
                            ps[:, 2 + k // 4, (k % 4) * P:(k % 4 + 1) * P], MUL, ADD)
                i.then_inc(hn_out, 1)
            dve.wait_ge(ys_full, NB)
            c.link(tt(yoff_s[:], eaE[:, :, P:P + TS], ps[:, 4, 0:SC * TS].rearrange("p (c x) -> p c x", c=SC), MUL))
            c.link(tt(yT[:, :, SEQ:T], yT[:, :, SEQ:T], yoff_s[:], ADD))
            dve.wait_ge(z_silu, 1)
            tt(yT[:], yT[:], proj[:, ZP:ZP + SC, :], MUL).then_inc(y_gated, 1)
            dve.wait_ge(y_gated, 1)
            for g in range(G):
                i = normed(yT[:, g * GCH:(g + 1) * GCH], yT[:, g * GCH:(g + 1) * GCH], rg[:, g], GCH)
            i.then_inc(y_normed, 1)
            dve.wait_ge(y_normed, 1)
            dve.wait_ge(y_hi, 1)
            for k in range(SC):
                i = stt(ylo[:, k, :], yT[:, k, :], vecT[:, 1, V_GS + k:V_GS + k + 1], yhi[:, k, :].bitcast(F32), MUL, SUB)
            i.then_inc(y_lo, 1)

            pairs(2, 4)
            ada_out(4)
            dve.wait_ge(ada_free, 24)

            def add_branch(m, gate, g):
                c.mark(normed(m[:], m[:], rT[:], KC))
                c.link(gain(gate, g, 0.0))
                c.link(tt(smp(m), smp(m), per_seq(gainT), MUL))
                for k in range(KC):
                    stt(xT[:, k, 0:SEQ], m[:, k, 0:SEQ], gainT[:, k, 0:1], xT[:, k, 0:SEQ], MUL, ADD)
                tt(smp(xT), smp(xT), smp(m), ADD).then_inc(x2_ready, 1)

            add_branch(mT, G1, V_POST_MIX)
            dve.wait_ge(x2_ready, 1)
            prepare(h2f, xT, SC2, SH2, V_PRE_FFN, 2)
            low(h2lo, h2f, h2hi, 2)

            dve.wait_ge(g2, 1)

            def taps_of(r):
                cols = vecT[:, 2:6, 0:2 * FC].rearrange("p v (s k) -> p v s k", s=2)[:, :, :, ds(r * MC, MC)]
                c.link(cp(fw[:], cols))

            def conv(r, s):
                u, o = ((ug, cg), (uv, cv))[s]
                W = UP - 2
                dve.wait_ge(f_u, 2 * r + s + 1)
                dve.wait_ge(f_ctx, 2 * r + s + 1)
                for k in range(MC):
                    i = ts(o[:, k, 0:W], u[:, k, 2:UP], fw[:, 3, s, k:k + 1], fw[:, 0, s, k:k + 1], MUL, ADD)
                c.link(i)
                for k in range(MC):
                    i = stt(o[:, k, 0:W], u[:, k, 1:1 + W], fw[:, 2, s, k:k + 1], o[:, k, 0:W], MUL, ADD)
                c.link(i)
                for k in range(MC):
                    i = stt(o[:, k, 0:W], u[:, k, 0:W], fw[:, 1, s, k:k + 1], o[:, k, 0:W], MUL, ADD)
                i.then_inc(f_c, 1)

            def product(r):
                dve.wait_ge(f_s, r + 1)
                dve.wait_ge(f_c, 2 * r + 2)
                if not (isinstance(r, int) and r == 0):
                    dve.wait_ge(f_lo, r)
                tt(gt[:, :, 0:SEQ], cg[:, :, 0:SEQ], cv[:, :, 0:SEQ], MUL)
                tt(smp(gt), own(cg), own(cv), MUL).then_inc(f_gt, 1)

            def own(a):
                return a[:, :, SEQ + 2:UP].rearrange("p m (b t) -> p m b t", b=NB)[:, :, :, 0:LS]

            def low_g(r):
                dve.wait_ge(f_hi, r + 1)
                tt(glo[:], gt[:], ghi[:].bitcast(F32), SUB).then_inc(f_lo, 1)

            def add(n, base):
                dve.wait_ge(w_used, base + n + 1)
                b = 4 * (n % 2)
                tt(fT[:, n * MC:(n + 1) * MC, :], fT[:, n * MC:(n + 1) * MC, :], ps[:, b:b + 4, 0:T], ADD).then_inc(f_add, 1)

            def round_(r, out, added):
                taps_of(r)
                lo(0)
                if added:
                    add(3, 4 * pos.split - 4)
                lo(1)
                if out:
                    low_g(r - 1)
                lo(2)
                lo(3)
                pos.step(quad=1, split=1)
                lo(0)
                lo(1)
                conv(r, 0)
                lo(2)
                lo(3)
                pos.step(quad=1, split=1)
                if out:
                    lo(0)
                    lo(1)
                conv(r, 1)
                if out:
                    add(0, 4 * pos.split)
                    lo(2)
                product(r)
                if out:
                    add(1, 4 * pos.split)
                    lo(3)
                    add(2, 4 * pos.split)
                    pos.step(quad=1, split=1)

            ROUNDS = FC // MC
            round_(0, False, False)
            round_(1, True, False)
            with dve.Fori(2, ROUNDS) as r:
                pos.enter(r, 2, quad=3, split=3)
                c.enter(r, 2, 5)
                round_(r, True, True)
                c.leave(ROUNDS - 2)
                pos.leave(ROUNDS - 2)
            add(3, 4 * pos.split - 4)
            low_g(ROUNDS - 1)
            for n in range(4):
                lo(n)
                if n >= 1:
                    add(n - 1, 4 * pos.split)
            add(3, 4 * pos.split)
            dve.wait_ge(f_add, 4 * ROUNDS)
            add_branch(fT, G2, V_POST_FFN)
            for n in range(4 * (NT + 1)):
                t, g = divmod(n, 4)
                w = P if t < NT else TS
                dve.wait_ge(ys_T, n + 1)
                cp(ystage[0:w, t, g * GC:(g + 1) * GC], ps[0:w, n % 8, :]).then_inc(ys_o, 1)


_INS = ['x_prompt', 'x_sample', 'c_prompt', 'c_sample', 'cache_k', 'cache_v', 'page_table', 'state_ssm', 'state_conv',
        'state_ffn_conv', 'w_ada', 'b_ada', 'g_pre_mix', 'g_post_mix', 'g_pre_ffn', 'g_post_ffn', 'w_in', 'conv_w',
        'conv_b', 'dt_bias', 'a_log', 'd_skip', 'g_ssd_norm', 'sb_bias', 'w_out', 'w_ffn_in', 'ffn_conv_w',
        'ffn_conv_b', 'w_ffn_out']
_OUTS = [(1, 256, 2048), (8, 4, 2048), (1, 1, 256, 8, 128), (1, 1, 256, 8, 128), (1, 1, 16, 64, 128), (1, 1, 3, 1536),
         (1, 1, 2, 11264), (1, 8, 4, 8, 128), (1, 8, 4, 8, 128), (1, 8, 16, 64, 128), (1, 8, 3, 1536), (1, 8, 2, 11264)]


def kernel(**inputs):
    import numpy as _np
    import concourse.bacc as _bacc
    from concourse import mybir as _mybir
    from concourse.bass_utils import run_bass_kernel_spmd as _run

    nc = _bacc.Bacc("TRN2", target_bir_lowering=False, num_devices=1)
    arrays, args = {}, []
    for name in _INS:
        a = _np.ascontiguousarray(inputs[name])
        arrays[f"in_{name}_dram"] = a
        args.append(nc.dram_tensor(f"in_{name}_dram", a.shape, _mybir.dt.from_np(a.dtype), kind="ExternalInput").ap())
    for i, shape in enumerate(_OUTS):
        args.append(nc.dram_tensor(f"out_{i}_dram", shape, _mybir.dt.float32, kind="ExternalOutput").ap())
    hybrid_step(nc, *args)
    r = _run(nc, [arrays], core_ids=[0])
    return tuple(r.results[0][f"out_{i}_dram"] for i in range(len(_OUTS)))
```

```python
from contextlib import ExitStack

import concourse.bass as bass
from concourse import mybir

F32 = mybir.dt.float32
F32R = mybir.dt.float32r
I32 = mybir.dt.int32
ALU = mybir.AluOpType
ACT = mybir.ActivationFunctionType
ds = bass.ds

P = 128
SSD_CHUNK = 128
KCONV = 4
KFFN = 3
EPS = 1e-6
MC = 4
GC = MC * P
QC = 4
RING = 4


class Count:

    def __init__(self, eng, sem):
        self.eng, self.sem, self.base, self.n = eng, sem, 0, 0

    def mark(self, ins):
        self.n += 1
        ins.then_inc(self.sem, 1)

    def value(self):
        return self.base + self.n

    def settle(self):
        self.eng.wait_ge(self.sem, self.value())

    def link(self, ins):
        self.mark(ins)
        self.settle()

    def enter(self, i, first, per):
        self.outer, self.per = self.value(), per
        self.base, self.n = (i - first) * per + self.outer, 0

    def leave(self, turns):
        assert self.n == self.per, (self.n, self.per)
        self.base, self.n = self.outer + turns * self.per, 0


class Place:

    KEYS = ("quad", "group", "ada")

    def __init__(self):
        self.base = dict.fromkeys(self.KEYS, 0)
        self.off = dict.fromkeys(self.KEYS, 0)

    @property
    def quad(self):
        return self.base["quad"] + self.off["quad"]

    @property
    def group(self):
        return self.base["group"] + self.off["group"]

    @property
    def ada(self):
        return self.base["ada"] + self.off["ada"]

    def step(self, **by):
        for k, v in by.items():
            self.off[k] += v

    def enter(self, i, first, **per):
        self.outer = {k: self.base[k] + self.off[k] for k in self.KEYS}
        self.per = {k: per.get(k, 0) for k in self.KEYS}
        self.base = {k: (i - first) * self.per[k] + self.outer[k] if self.per[k] else self.outer[k] for k in self.KEYS}
        self.off = dict.fromkeys(self.KEYS, 0)

    def leave(self, turns):
        assert self.off == self.per, (self.off, self.per)
        self.base = {k: self.outer[k] + turns * self.per[k] for k in self.KEYS}
        self.off = dict.fromkeys(self.KEYS, 0)


def hybrid_step(nc, x_prompt, x_sample, c_prompt, c_sample, cache_k, cache_v, page_table, state_ssm, state_conv,
                state_ffn_conv, w_ada, b_ada, g_pre_mix, g_post_mix, g_pre_ffn, g_post_ffn, w_in, conv_w, conv_b,
                dt_bias, a_log, d_skip, g_ssd_norm, sb_bias, w_out, w_ffn_in, ffn_conv_w, ffn_conv_b, w_ffn_out,
                y_prompt, y_sample, k_prompt, v_prompt, ssm_prompt, conv_prompt, ffn_conv_prompt,
                k_sample, v_sample, ssm_sample, conv_sample, ffn_conv_sample):
    _, SEQ, DM = x_prompt.shape
    NB, LS, _ = x_sample.shape
    TS = NB * LS
    T = SEQ + TS
    NT = SEQ // P
    KC = DM // P
    _, _, HS, PD, NS = state_ssm.shape
    DSSD = HS * PD
    SC = DSSD // P
    CD = conv_w.shape[2]
    XC = CD // P
    G = (CD - DSSD) // (2 * NS)
    GCH = SC // G
    _, NPOOL, PAGE, HA, DH = cache_k.shape
    DATT = HA * DH
    AC = DATT // P
    NPG = page_table.shape[1]
    DFF = w_ffn_out.shape[1]
    FC = DFF // P
    NSEQ = NB + 1
    MODC = 6 * KC
    SCALE = float(DH) ** -0.5
    ZP, XP, QP, KP, VP = 0, SC, SC + XC, SC + XC + AC, SC + XC + 2 * AC
    PC = SC + XC + 3 * AC
    COL_DT = DSSD + CD
    COL_Q = COL_DT + HS
    ZX_GROUPS = (SC + XC) // MC
    QKV_GROUPS = 3 * AC // MC
    PROJ_QUADS = 8 + 2 * (ZX_GROUPS + QKV_GROUPS)
    HQ = HA * LS
    assert NT == 2 and TS == 32 and SEQ == 256 and PD == 64 and NS == P and DH == P and PAGE == P
    assert ZX_GROUPS == 5 and QKV_GROUPS == 6 and KC == 16 and FC % MC == 0 and G == 2 and NPG == 8

    ctx = ExitStack()
    with ctx:
        BASE = -(-nc.sbuf_base // 32) * 32
        at = lambda name, shape, off, dt=F32: nc.alloc_sbuf_tensor_at(name, shape, dt, offset=BASE + off)
        CH = T * 4
        raw = at("raw", [P, RING, QC, GC], 0)
        WREG = RING * QC * GC * 4
        whi = at("whi", [P, 2, QC, GC], WREG, F32R)
        wlo = at("wlo", [P, 2, QC, GC], WREG + 16384, F32R)
        cur = [WREG + 32768]

        def keep(name, shape, dt=F32):
            size = 4
            for d in shape[1:]:
                size *= d
            t = at(name, shape, cur[0], dt)
            cur[0] += -(-size // 32) * 32
            return t

        xT = keep("xT", [P, KC, T])
        modT = keep("modT", [P, MODC, NSEQ])
        vecT = keep("vecT", [P, 6, P])
        ctxT = keep("ctxT", [P, 2 * FC, NB * (KFFN - 1)])
        xpad = keep("xpad", [P, XC, NB, LS + KCONV - 1])
        ident = keep("ident", [P, P])
        ones = keep("ones", [P, P])
        incl = keep("incl", [P, P])
        later = keep("later", [P, P])
        cmask = keep("cmask", [P, 3 * P])
        sel = keep("sel", [HS, SC, P])
        zbias = keep("zbias", [P, NPG, HA, LS])
        cs = keep("cs", [P, KC, 2 * NSEQ], F32R)
        small = keep("small", [P, 4 + HA + SC + NSEQ])
        dtb, nega, dskip, eps = (small[0:n, i:i + 1] for i, n in enumerate((HS, HS, HS, P)))
        sbb, dskE = small[:, 4:4 + HA], small[:, 4 + HA:4 + HA + SC]
        hi_and_lo = small[0:2 * NSEQ, 4 + HA + SC:]
        incl_s = keep("incl_s", [TS, TS])
        later_s = keep("later_s", [TS, TS])
        before_s = keep("before_s", [TS, TS])
        seq_of = keep("seq_of", [TS, NB])
        gainT = keep("gainT", [P, KC, NSEQ])
        rT = keep("rT", [P, T])
        ptab = keep("ptab", [1, NB * NPG], I32)
        dA_tok = keep("dA_tok", [P, NT + 1, HS])
        ac_tok = keep("ac_tok", [P, NT + 1, HS])
        dend_tok = keep("dend_tok", [P, NT + 2, HS])
        D = cur[0]
        room = nc.sbuf_usable_end - BASE - D
        assert room >= 99840 + CH, room

        hhi = at("hhi", [P, KC, T], D, F32R)
        hlo = at("hlo", [P, KC, T], D + 16 * CH, F32R)
        sq0 = at("sq0", [P, KC, T], D)
        proj = at("proj", [P, PC, T], D + 32 * CH)
        xrow = at("xrow", [P, NT + 1, DM], D + 32 * CH)
        vrow = at("vrow", [P, 6, P], D + 61440)
        crow = at("crow", [NSEQ, DM], D + 64512)
        frow = at("frow", [P, 11, P], D + 72704)
        srow = at("srow", [P, 3, P], D + 78336)
        hf = at("hf", [P, KC, T], D + 32 * CH + KP * CH)
        wdt = at("wdt", [P, KC, HS], D + 87552)
        arow = at("arow", [2 * NSEQ, GC], D + 89600)
        cT = at("cT", [P, KC, NSEQ], D + 92160)
        dtraw = at("dtraw", [HS, T], D + 99840)
        kring = at("kring", [P, 4, HA, DH], D)
        vring = at("vring", [P, 4, HA, DH], D + 16384)
        kstage = at("kstage", [P, DATT], D + 32768)
        vtok = at("vtok", [P, NT + 1, DATT], D + 87552)
        kt = at("kt", [P, 2, HA, P], WREG)
        oT = at("oT", [P, AC, T], WREG + 8192)
        pz, pa, psp, pspm, pw = (at(n, [P, 3 * P], WREG + 17408 + 1536 * i)
                                 for i, n in enumerate(("pz", "pa", "psp", "pspm", "pw")))
        o_new = at("o_new", [P, HA, TS], WREG + 25088)
        dz, da, dsp, dw = (at(n, [P, NPG, HA, LS], WREG + 26624 + 1024 * i)
                           for i, n in enumerate(("dz", "da", "dsp", "dw")))
        ccol = at("ccol", [P, 3, 27, 4], WREG + 26624)
        cout = at("cout", [27 * 4, 3, P], WREG + 26624 + 1536)
        zrow = at("zrow", [HQ, 2, NPG // 2, P], WREG + 17408)
        later_pages = at("later_pages", [P, NPG, HA, LS], WREG + 21504)
        qmask = at("qmask", [P, HA * (HQ + LS)], WREG + 22528)
        orow = at("orow", [LS, DATT], D + 32768)
        sp_new = at("sp_new", [TS, HA, TS], WREG + 30848)
        xc = at("xc", [P, XC, T], D)
        xdt_tok = at("xdt_tok", [P, NT + 1, DSSD], D + 13824)
        xdtT = at("xdtT", [P, SC, T], D + 26112)
        xde_s = at("xde_s", [TS, DSSD], D + 26112)
        B_tok = at("B_tok", [P, NT + 1, G, NS], D + 30208)
        yoff_s = at("yoff_s", [P, SC, TS], D + 35328)
        xde = at("xde", [P, 3, DSSD], D + 46080)
        yT = at("yT", [P, SC, T], D + 59904)
        ohi = at("ohi", [P, AC, T], D + 69120, F32R)
        olo = at("olo", [P, AC, T], D + 78336, F32R)
        h0 = at("h0", [P, 2, SC, NS], D + 87552)
        h0T = at("h0T", [P, SC, P], D + 95744)
        hb = at("hb", [HS, HS, P], WREG)
        hnew = at("hnew", [P, 2, SC, NS], WREG)
        eaE = at("eaE", [P, SC, P + TS], WREG + 8192)
        cbm = at("cbm", [P, G, T], WREG + 13312)
        seg = at("seg", [P, 2, T], WREG + 15616)
        dec = at("dec", [P, 2, T], WREG + 17920)
        sco = at("sco", [P, 2, T], WREG + 20224)
        h1T = at("h1T", [P, DSSD], WREG + 22528)
        dtT, dA_T, acT, t1, t2 = (at(n, [HS, T], WREG + 26624 + CH * i)
                                  for i, n in enumerate(("dtT", "dA_T", "acT", "t1", "t2")))
        bm_s = at("bm_s", [TS, G, NS], D + 33280)
        ctmp = at("ctmp", [P, XC, TS], D + 13824)
        ytmp = at("ytmp", [P, SC, P], WREG + 15616)
        rg = at("rg", [P, G, T], WREG + 22528)
        sq1 = at("sq1", [P, SC, T], D + 46080)
        yhi = at("yhi", [P, SC, T], D, F32R)
        ylo = at("ylo", [P, SC, T], D + SC * CH, F32R)
        mT = at("mT", [P, KC, T], D + 16 * CH)
        sq2 = at("sq2", [P, KC, T], D + 32 * CH)
        h2f = at("h2f", [P, KC, T], D + 48 * CH)
        h2hi = at("h2hi", [P, KC, T], D, F32R)
        h2lo = at("h2lo", [P, KC, T], D + 16 * CH, F32R)
        fT = at("fT", [P, KC, T], D + 32 * CH)
        UP = SEQ + KFFN - 1 + NB * (LS + KFFN - 1)
        ghi = at("ghi", [P, MC, T], D + 55296, F32R)
        glo = at("glo", [P, MC, T], D + 59904, F32R)
        fw = at("fw", [P, 4, 2, MC], D + 64512)
        ug = at("ug", [P, MC, UP], D + 73728)
        uv = at("uv", [P, MC, UP], D + 78624)
        cg = at("cg", [P, MC, UP], D + 83520)
        cv = at("cv", [P, MC, UP], D + 88416)
        pcol = at("pcol", [P, 2 * FC, 2], D + 93312)
        gt = at("gt", [P, MC, T], D + 94016)
        fcomp = at("fcomp", [P, 11, P], D + 55296)
        sq3 = at("sq3", [P, KC, T], D)
        ystage = at("ystage", [P, NT + 1, DM], D + 55296)
        fstage = at("fstage", [P, 11, P], D + 79872)
        fpstage = at("fpstage", [2 * FC, 2, P], D + 85504)

        ps = ctx.enter_context(nc.psum_tensor("ps", [P, 8, 512], F32))

        def sem(name):
            return ctx.enter_context(nc.semaphore(name))

        raw_full = [sem(f"raw_full{j}") for j in range(RING)]
        hi_ready, lo_ready, w_used = sem("hi_ready"), sem("lo_ready"), sem("w_used")
        group_free = sem("group_free")
        ada_row, fold_full, mod_ready = sem("ada_row"), sem("fold_full"), sem("mod_ready")
        cs_hi, cs_ready = sem("cs_hi"), sem("cs_ready")
        in_c, in_vec, in_ctx, in_x, in_misc, in_pt = (sem(n) for n in ("in_c", "in_vec", "in_ctx", "in_x", "in_misc", "in_pt"))
        consts = sem("consts")
        pool_c, act_c, dve_c = sem("pool_c"), sem("act_c"), sem("dve_c")
        rows_T = sem("rows_T")
        rows_out = sem("rows_out")
        x_T, x_out = sem("x_T"), sem("x_out")
        c_ready = sem("c_ready")
        sq_ready, sum_ready, root_ready = sem("sq_ready"), sem("sum_ready"), sem("root_ready")
        xr_ready, hp_ready, hs_ready = sem("xr_ready"), sem("hp_ready"), sem("hs_ready")
        h_hi, h_lo = sem("h_hi"), sem("h_lo")
        dt_full, dt_out = sem("dt_full"), sem("dt_out")
        tok_full, ktok_out, vtok_out, tok_dma = sem("tok_full"), sem("ktok_out"), sem("vtok_out"), sem("tok_dma")
        ccol_ready, ccol_T, ccol_out, ccol_dma = sem("ccol_ready"), sem("ccol_T"), sem("ccol_out"), sem("ccol_dma")
        z_full, z_e, z_sp, tail_full, w_e, w_ready, o_full, o_out = (
            sem(n) for n in ("z_full", "z_e", "z_sp", "tail_full", "w_e", "w_ready", "o_full", "o_out"))
        z_na = sem("z_na")
        w_d = sem("w_d")
        kfull = [sem(f"kfull{j}") for j in range(4)]
        vfull = [sem(f"vfull{j}") for j in range(4)]
        kT_full, kT_act, kT_dve = sem("kT_full"), sem("kT_act"), sem("kT_dve")
        zrow_out, z_T, dn_suffix, orow_out, o_T = (sem(n) for n in ("zrow_out", "z_T", "dn_suffix", "orow_out", "o_T"))
        qb_ready, page_scored, page_summed = sem("qb_ready"), sem("page_scored"), sem("page_summed")
        dn_na, dn_e, dn_sp, dtail_full, dn_d, dn_w, do_out = (
            sem(n) for n in ("dn_na", "dn_e", "dn_sp", "dtail_full", "dn_d", "dn_w", "do_out"))
        ov_hi, ov_lo = sem("ov_hi"), sem("ov_lo")
        conv_done, silu_done = sem("conv_done"), sem("silu_done")
        g2 = sem("g2")
        hb_ready = sem("hb_ready")
        bc_full, seg_ready, dec_ready, sco_ready, yd_full, yd_out = (
            sem(n) for n in ("bc_full", "seg_ready", "dec_ready", "sco_ready", "yd_full", "yd_out"))
        h0_full = [sem(f"h0_full{j}") for j in range(2)]
        h0T_full, h0T_out, bm_ready, hn_full, hn_out, ys_full = (
            sem(n) for n in ("h0T_full", "h0T_out", "bm_ready", "hn_full", "hn_out", "ys_full"))
        hn_dma = [sem(f"hn_dma{j}") for j in range(2)]
        y_hi, y_lo = sem("y_hi"), sem("y_lo")
        x2_ready = sem("x2_ready")
        f_u, f_c, f_s, f_gt, f_hi, f_lo, f_ctx, f_col = (
            sem(n) for n in ("f_u", "f_c", "f_s", "f_gt", "f_hi", "f_lo", "f_ctx", "f_col"))
        fcomp_ready = sem("fcomp_ready")
        ys_T, ys_o, out_dma = sem("ys_T"), sem("ys_o"), sem("out_dma")
        fc_T, fc_o = sem("fc_T"), sem("fc_o")
        (dt_na, dt_e, dt_ln, dt_done, a_ready, dA_full, dA_ready, ac_full, ac_out, ac_exp, xdt_made, dtE_full, eaE_made,
         acE_full, xdt_full, xdt_out, B_full, B_out, cb_full, cbm_made, xde_made, h1_full, h1_out, yo_full, yo_out,
         z_silu, y_gated, ysq_ready, y_normed, f_add) = (
            sem(n) for n in ("dt_na", "dt_e", "dt_ln", "dt_done", "a_ready", "dA_full", "dA_ready", "ac_full", "ac_out",
                             "ac_exp", "xdt_made", "dtE_full", "eaE_made", "acE_full", "xdt_full", "xdt_out", "B_full",
                             "B_out", "cb_full", "cbm_made", "xde_made", "h1_full", "h1_out", "yo_full", "yo_out",
                             "z_silu", "y_gated", "ysq_ready", "y_normed", "f_add"))
        ssm_dma, ssm_full, ssm_out = sem("ssm_dma"), sem("ssm_full"), sem("ssm_out")

        w_ada_v, w_in_v, w_out_v, w_fi_v, w_fo_v = w_ada[0], w_in[0], w_out[0], w_ffn_in[0], w_ffn_out[0]

        SH1, SC1, G1, SH2, SC2, G2 = (k * KC for k in range(6))
        V_PRE_MIX, V_POST_MIX = (0, MODC), (0, MODC + KC)
        V_PRE_FFN, V_POST_FFN = (1, 0), (1, KC)
        V_CW, V_CB, V_GS = 2 * KC, 2 * KC + KCONV * XC, 2 * KC + (KCONV + 1) * XC

        def smp(ap):
            return ap[:, :, SEQ:T].rearrange("p n (b t) -> p n b t", b=NB)

        block = ctx.enter_context(nc.Block())

        @block.sync
        def _(sp):
            pos = Place()

            def quad(src):
                for j in range(RING):
                    if not (isinstance(pos.quad, int) and pos.quad == 0):
                        sp.wait_ge(lo_ready, 4 * (pos.quad - 1) + j + 1)
                    sp.dma_start(raw[:, j], src(j)).then_inc(raw_full[j], 16)
                pos.step(quad=1)

            def rows(w, j, col):
                return w[j * QC * P:(j + 1) * QC * P, ds(col, GC)].rearrange("(q p) n -> p q n", p=P)

            def ada():
                quad(lambda j: rows(w_ada_v, j, pos.ada * GC))
                pos.step(ada=1)

            def proj_in(col):
                quad(lambda j: rows(w_in_v, j, col))

            ada()
            with sp.Fori(1, 8) as i:
                pos.enter(i, 1, quad=1, ada=1)
                ada()
                pos.leave(7)
            proj_in(0)
            ada()
            with sp.Fori(0, 2) as i:
                pos.enter(i, 0, quad=4, ada=2)
                for half in range(2):
                    proj_in(i * (2 * GC) + (half + 1) * GC)
                    ada()
                pos.leave(2)
            with sp.Fori(0, 3) as i:
                pos.enter(i, 0, quad=4, ada=2)
                for half in range(2):
                    proj_in(i * (2 * GC) + half * GC + COL_Q)
                    ada()
                pos.leave(3)

            sp.wait_ge(w_used, 4 * PROJ_QUADS)
            sp.wait_ge(in_pt, 16)

            def k_page(b, p):
                if not (isinstance(b, int) and b * NPG + p < 4):
                    sp.wait_ge(kT_full, b * NPG + p - 3)
                pg = sp.value_load(ptab[0:1, ds(b * NPG + p, 1)], min_val=0, max_val=NPOOL - 1)
                sp.dma_start(kring[:, p % 4], cache_k[0][ds(pg, 1)].rearrange("o k h d -> (o k) h d"))\
                    .then_inc(kfull[p % 4], 16)

            def v_page(b, p):
                if not (isinstance(b, int) and b * NPG + p < 4):
                    sp.wait_ge(page_summed, b * NPG + p - 3)
                pg = sp.value_load(ptab[0:1, ds(b * NPG + p, 1)], min_val=0, max_val=NPOOL - 1)
                sp.dma_start(vring[:, p % 4], cache_v[0][ds(pg, 1)].rearrange("o k h d -> (o k) h d"))\
                    .then_inc(vfull[p % 4], 16)

            for p in range(NPG):
                k_page(0, p)
            for p in range(NPG):
                k_page(1, p)
                v_page(0, p)
            with sp.Fori(2, NB) as b:
                for p in range(NPG):
                    k_page(b, p)
                    v_page(b - 1, p)
            for p in range(NPG):
                v_page(NB - 1, p)

            sp.wait_ge(o_out, 1 + HA)
            sp.wait_ge(tok_dma, 16 * 6)
            for b in range(NB):
                if b >= 2:
                    sp.wait_ge(hn_out, b - 1)
                sp.dma_start(h0[:, b % 2], state_ssm[0, b].rearrange("(c a) d n -> (a d) c n", a=P // PD))\
                    .then_inc(h0_full[b % 2], 16)

            ada()
            with sp.Fori(0, 2) as i:
                pos.enter(i, 0, quad=4, ada=2)
                for half in range(2):
                    quad(lambda j: rows(w_out_v, j, i * (2 * GC) + half * GC))
                    ada()
                pos.leave(2)

            def fo(r):
                def src(n):
                    return w_fo_v[ds(r * GC, GC), n * GC:(n + 1) * GC].rearrange("(q p) n -> p q n", p=P)
                quad(src)

            def round_(r, out):
                quad(lambda j: rows(w_fi_v, j, r * GC))
                quad(lambda j: rows(w_fi_v, j, r * GC + DFF))
                if out:
                    fo(r - 1)

            round_(0, False)
            round_(1, True)
            with sp.Fori(2, FC // MC) as r:
                pos.enter(r, 2, quad=3)
                round_(r, True)
                pos.leave(FC // MC - 2)
            fo(FC // MC - 1)

        @block.gpsimd
        def _(pool):
            c = Count(pool, pool_c)
            ge, fill = ALU.is_ge, 0.0
            for m, v in ((ident, 0.0), (hi_and_lo, 0.0), (ones, 1.0), (incl, 1.0), (later, 1.0), (cmask, 1.0), (sel, 1.0), (incl_s, 1.0),
                         (later_s, 1.0), (before_s, 1.0), (seq_of, 1.0)):
                c.mark(pool.memset(m[:], v))
            c.settle()

            def keep_where(m, pattern, base, cm):
                c.mark(pool.affine_select(out=m, in_=m, compare_op=ge, fill=fill, base=base, pattern=pattern,
                                          channel_multiplier=cm))

            c.mark(pool.affine_select(out=ident[:], in_=ident[:], compare_op=ALU.not_equal, fill=1.0, base=0,
                                      pattern=[[-1, P]], channel_multiplier=1))
            c.mark(pool.affine_select(out=hi_and_lo[:], in_=hi_and_lo[:], compare_op=ALU.not_equal, fill=1.0, base=0,
                                      pattern=[[-1, NSEQ]], channel_multiplier=1))
            keep_where(incl[:], [[1, P]], 0, -1)
            keep_where(later[:], [[-1, P]], -1, 1)
            keep_where(cmask[:, 0:P], [[1, P]], -1, -1)
            keep_where(cmask[:, 2 * P:3 * P], [[1, P]], -1, -1)
            keep_where(sel[:], [[P, SC], [1, P]], 0, -PD)
            keep_where(incl_s[:], [[1, TS]], 0, -1)
            keep_where(later_s[:], [[-1, TS]], -1, 1)
            keep_where(before_s[:], [[1, TS]], -1, -1)
            keep_where(seq_of[:], [[-LS, NB]], 0, 1)
            c.settle()
            keep_where(sel[:], [[-P, SC], [-1, P]], PD - 1, PD)
            c.mark(pool.affine_select(out=hi_and_lo[:], in_=hi_and_lo[:], compare_op=ALU.not_equal, fill=1.0, base=-NSEQ,
                                      pattern=[[-1, NSEQ]], channel_multiplier=1))
            keep_where(incl_s[:], [[-LS, NB], [0, LS]], 0, 1)
            keep_where(later_s[:], [[-LS, NB], [0, LS]], 0, 1)
            keep_where(before_s[:], [[-LS, NB], [0, LS]], 0, 1)
            keep_where(seq_of[:], [[LS, NB]], LS - 1, -1)
            c.settle()
            keep_where(incl_s[:], [[LS, NB], [0, LS]], LS - 1, -1)
            keep_where(later_s[:], [[LS, NB], [0, LS]], LS - 1, -1)
            keep_where(before_s[:], [[LS, NB], [0, LS]], LS - 1, -1)
            c.settle()
            c.link(pool.memset(eps[:], EPS))
            pool.memset(dA_tok[:], 0.0).then_inc(consts, 1)
            pool.memset(ac_tok[:], 0.0).then_inc(consts, 1)

            for n in range(2 * (NT + 1)):
                kind, t = divmod(n, NT + 1)
                src = kstage if kind == 0 else vtok
                pool.wait_ge((ktok_out, vtok_out)[kind], t + 1)
                if t < NT:
                    dst = (k_prompt, v_prompt)[kind][0, 0, t * P:(t + 1) * P].rearrange("t h d -> t (h d)")
                    piece = src[:, :] if kind == 0 else src[:, t, :]
                else:
                    dst = (k_sample, v_sample)[kind][0].rearrange("b t h d -> (b t) (h d)")
                    piece = src[0:TS, :] if kind == 0 else src[0:TS, t, :]
                pool.dma_start(dst, piece).then_inc(tok_dma, 16)
            pool.wait_ge(ccol_out, 1)
            pool.dma_start(conv_prompt[0, 0].rearrange("r (g x) -> (r g) x", g=4),
                           cout[0:12].rearrange("p c f -> p (c f)")).then_inc(ccol_dma, 16)
            pool.dma_start(conv_sample[0].rearrange("b r (g x) -> (b r g) x", g=4),
                           cout[12:108].rearrange("p c f -> p (c f)")).then_inc(ccol_dma, 16)

            pool.wait_ge(o_out, 1 + HA)
            c.link(pool.memset(qmask[:], 0.0))
            own = qmask[:].rearrange("p (h x) -> p h x", h=HA)[:, :, 0:LS]
            for b in range(NB):
                if b:
                    pool.wait_ge(page_scored, NPG * b)
                pool.tensor_copy(own, proj[:, QP:QP + AC, SEQ + LS * b:SEQ + LS * (b + 1)]).then_inc(qb_ready, 1)

            pool.wait_ge(ov_lo, 1)
            c.link(pool.memset(hb[:], 0.0))
            c.link(pool.affine_select(out=hb[:], in_=hb[:], compare_op=ALU.not_equal, fill=1.0, base=0,
                                      pattern=[[-1, HS], [0, P]], channel_multiplier=1))
            pool.memset(cbm[:], 0.0).then_inc(hb_ready, 1)

            pool.wait_ge(ssm_out, 1)
            pool.dma_start(ssm_prompt[0, 0].rearrange("(c a) d n -> (a d) c n", a=P // PD), hnew[:, 1]).then_inc(ssm_dma, 16)
            for b in range(NB):
                pool.wait_ge(hn_out, b + 1)
                pool.dma_start(ssm_sample[0, b].rearrange("(c a) d n -> (a d) c n", a=P // PD), hnew[:, b % 2])\
                    .then_inc(hn_dma[b % 2], 16)

            pool.wait_ge(h_lo, 2)
            for u in (ug, uv):
                c.mark(pool.memset(u[:, :, 0:KFFN - 1], 0.0))
            pool.memset(fT[:], 0.0).then_inc(g2, 1)
            c.settle()

            def upad(u, a, n):
                return u[:, :, SEQ + 2:UP].rearrange("p m (b t) -> p m b t", b=NB)[:, :, :, a:a + n]

            def contexts(r, first):
                for s, u in ((0, ug), (1, uv)):
                    chunks = ds(r * MC + s * FC, MC)
                    if not first:
                        pool.wait_ge(f_c, 2 * (r - 1) + s + 1)
                    pool.tensor_copy(upad(u, 0, 2), ctxT[:, chunks, :].rearrange("p m (b t) -> p m b t", b=NB))\
                        .then_inc(f_ctx, 1)
                for s, u in ((0, ug), (1, uv)):
                    chunks = ds(r * MC + s * FC, MC)
                    pool.wait_ge(f_u, 2 * r + s + 1)
                    pool.wait_ge(f_ctx, 2 * r + s + 1)
                    c.mark(pool.tensor_copy(ctxT[:, chunks, :].rearrange("p m (b t) -> p m b t", b=NB), upad(u, LS, 2)))
                    pool.tensor_copy(pcol[:, chunks, :], u[:, :, SEQ:SEQ + 2]).then_inc(f_col, 1)

            for r in range(FC // MC):
                contexts(r, r == 0)

            c.settle()
            pool.wait_ge(f_lo, FC // MC)
            pool.wait_ge(w_used, 4 * (PROJ_QUADS + 9 + 3 * FC // MC))
            pool.tensor_copy(fcomp[:].rearrange("p c (r g) -> p c r g", g=8),
                             ctxT[:].rearrange("p (g c) r -> p c r g", c=11)).then_inc(fcomp_ready, 1)
            pool.wait_ge(fc_o, 2)
            pool.dma_start(ffn_conv_sample[0].rearrange("b r (g x) -> (b r g) x", g=8),
                           fstage[:].rearrange("p c f -> p (c f)")).then_inc(out_dma, 16)
            for r in range(2):
                pool.dma_start(ffn_conv_prompt[0, 0, r].rearrange("(c f) -> c f", f=P), fpstage[:, r]).then_inc(out_dma, 16)
            for t in range(NT):
                pool.wait_ge(ys_o, 4 * (t + 1))
                pool.dma_start(y_prompt[0, t * P:(t + 1) * P], ystage[:, t]).then_inc(out_dma, 16)
            pool.wait_ge(ys_o, 4 * (NT + 1))
            pool.dma_start(y_sample.rearrange("b t d -> (b t) d"), ystage[0:TS, NT]).then_inc(out_dma, 16)
            pool.wait_ge(out_dma, 16 * 6)
            pool.wait_ge(tok_dma, 16 * 6)
            pool.wait_ge(ccol_dma, 32)
            pool.wait_ge(ssm_dma, 16)
            pool.wait_ge(hn_dma[0], 16 * (NB // 2))
            pool.wait_ge(hn_dma[1], 16 * (NB // 2))

        @block.tensor
        def _(pe):
            pos = Place()
            mm = nc.tensor.matmul

            def tr(out, in_, k):
                return nc.tensor.transpose(out, in_, ident[0:k, 0:k])

            def fold(bank):
                pe.wait_ge(ada_row, pos.ada)
                if not (isinstance(pos.ada, int) and pos.ada < 2):
                    pe.wait_ge(mod_ready, pos.ada - 1)
                for m in range(MC):
                    i = mm(ps[:, bank + 2, m * NSEQ:(m + 1) * NSEQ], arow[:, m * P:(m + 1) * P], hi_and_lo[:],
                           start=True, stop=True)
                i.then_inc(fold_full, 1)

            def adaq(bank, fold_last=True):
                pe.wait_ge(group_free, pos.group + 1)
                if fold_last:
                    fold(bank)
                for j in range(RING):
                    pe.wait_ge(lo_ready, 4 * pos.quad + j + 1)
                    for q in range(QC):
                        k = j * QC + q
                        o = ps[0:2 * NSEQ, bank + 3, :]
                        mm(o, cs[:, k, :], whi[:, j % 2, q, :], start=(k == 0), stop=False)
                        i = mm(o, cs[:, k, :], wlo[:, j % 2, q, :], start=False, stop=(k == KC - 1))
                    i.then_inc(w_used, 1)
                pos.step(quad=1, ada=1)

            def unit3(j, bank0, xs, first, last, before=lambda m: None):
                s = j % 2
                for m in range(MC):
                    before(m)
                    for q in range(QC):
                        xh, xl = xs(q)
                        o = ps[:, bank0 + m, 0:T]
                        cols = slice(m * P, (m + 1) * P)
                        mm(o, whi[:, s, q, cols], xh, start=(first and q == 0), stop=False)
                        mm(o, whi[:, s, q, cols], xl, start=False, stop=False)
                        i = mm(o, wlo[:, s, q, cols], xh, start=False, stop=(last and q == QC - 1))
                return i

            def group(bank0, xhi, xlo):
                pe.wait_ge(group_free, pos.group + 1)

                def ada_gone(m):
                    if m == 2:
                        pe.wait_ge(mod_ready, pos.ada - 1)
                    if m == 3:
                        pe.wait_ge(ada_row, pos.ada)

                for j in range(RING):
                    pe.wait_ge(lo_ready, 4 * pos.quad + j + 1)
                    i = unit3(j, bank0, lambda q: (xhi(j * QC + q), xlo(j * QC + q)), j == 0, j == RING - 1,
                              ada_gone if j == 0 else (lambda m: None))
                    i.then_inc(w_used, 1)
                pos.step(quad=1, group=1)

            pe.wait_ge(pool_c, 31)
            pe.wait_ge(in_vec, 16 * 10)
            for n in range(6):
                k = P if n == 0 else (2 * KC + (KCONV + 1) * XC + SC if n == 1 else 2 * FC)
                i = tr(ps[:, n // 4, (n % 4) * P:(n % 4) * P + k], vrow[0:k, n, :], k)
            i.then_inc(rows_T, 1)
            pe.wait_ge(in_c, 32)
            for k in range(KC):
                i = tr(ps[:, 1, 256 + k * NSEQ:256 + (k + 1) * NSEQ], crow[:, k * P:(k + 1) * P], NSEQ)
            i.then_inc(rows_T, 1)
            pe.wait_ge(in_ctx, 32)
            for n in range(11):
                i = tr(ps[:, 2 + n // 4, (n % 4) * P:(n % 4 + 1) * P], frow[:, n, :], P)
            i.then_inc(rows_T, 1)
            for n in range(3):
                i = tr(ps[:, 5, n * 96:(n + 1) * 96], srow[0:96, n, :], 96)
            i.then_inc(rows_T, 1)
            pe.wait_ge(in_x, 48)
            for n in range(12):
                t, g = divmod(n, 4)
                k = P if t < NT else TS
                if n == 2:
                    pe.wait_ge(rows_out, 1)
                    pe.wait_ge(c_ready, 1)
                if n >= 8:
                    pe.wait_ge(x_out, n - 7)
                for m in range(4):
                    c0 = (g * 4 + m) * P
                    i = tr(ps[:, (6 + n) % 8, m * k:(m + 1) * k], xrow[0:k, t, c0:c0 + P], k)
                i.then_inc(x_T, 1)

            norms = [0]

            def sums(sq, chunks, bank):
                for n, k in enumerate(chunks):
                    i = mm(ps[:, bank, 0:T], ones[:], sq[:, k, :], start=(n == 0), stop=(n == len(chunks) - 1))
                i.then_inc(sum_ready, 1)

            def norm_sums(sq):
                norms[0] += 1
                pe.wait_ge(sq_ready, norms[0])
                sums(sq, range(KC), 2)

            pe.wait_ge(x_out, 12)
            norm_sums(sq0)
            pe.wait_ge(cs_ready, 1)
            adaq(4, fold_last=False)
            with pe.Fori(1, 8) as i_:
                pos.enter(i_, 1, quad=1, ada=1)
                adaq(4)
                pos.leave(7)
            fold(4)

            pe.wait_ge(in_misc, 16 * 5)
            pe.wait_ge(hp_ready, 1)
            pe.wait_ge(hs_ready, 1)
            for k in range(KC):
                i = mm(ps[0:HS, 7, 0:T], wdt[:, k, :], hf[:, k, :], start=(k == 0), stop=(k == KC - 1))
            i.then_inc(dt_full, 1)
            pe.wait_ge(h_lo, 1)
            pe.wait_ge(dt_out, 1)

            def pair(bank0, xh, xl, fold_last=True):
                group(bank0, xh, xl)
                adaq(4 - bank0, fold_last)

            def pairs(turns, bank0, xh, xl):
                with pe.Fori(0, turns) as i_:
                    pos.enter(i_, 0, quad=4, group=2, ada=2)
                    pair(bank0, xh, xl)
                    pair(4 - bank0, xh, xl)
                    pos.leave(turns)

            hx = (lambda k: hhi[:, k, :]), (lambda k: hlo[:, k, :])
            pair(0, *hx, fold_last=False)
            pairs(2, 4, *hx)
            pairs(3, 4, *hx)
            fold(4)

            pe.wait_ge(group_free, 2 + ZX_GROUPS + QKV_GROUPS)
            pe.wait_ge(mod_ready, 8 + ZX_GROUPS + QKV_GROUPS)
            for n in range(2 * (NT + 1)):
                kind, t = divmod(n, NT + 1)
                w = P if t < NT else TS
                if n >= 2:
                    pe.wait_ge((ktok_out, vtok_out)[(n - 2) // 3], (n - 2) % 3 + 1)
                for h in range(HA):
                    i = tr(ps[0:w, 2 * (n % 2) + h // 4, (h % 4) * P:(h % 4 + 1) * P],
                           proj[:, (KP, VP)[kind] + h, t * P:t * P + w], P)
                i.then_inc(tok_full, 1)
            pe.wait_ge(ccol_ready, 1)
            for c in range(3):
                i = tr(ps[0:108, 7, c * P:(c + 1) * P], ccol[:, c].rearrange("p r g -> p (r g)"), P)
            i.then_inc(ccol_T, 1)

            for h in range(HA):
                i = mm(ps[0:TS, 4, h * TS:(h + 1) * TS], proj[:, KP + h, SEQ:T], proj[:, QP + h, SEQ:T],
                       start=True, stop=True)
            i.then_inc(z_full, 1)
            pe.wait_ge(z_sp, 1)
            mm(ps[0:TS, 5, 0:HA * TS], later[0:TS, 0:TS], sp_new[:].rearrange("p h t -> p (h t)"), start=True, stop=True)\
                .then_inc(tail_full, 1)
            pe.wait_ge(w_ready, 1)
            pe.wait_ge(vtok_out, 3)
            for h in range(HA):
                i = mm(ps[:, 6, h * TS:(h + 1) * TS], vtok[0:TS, NT, h * DH:(h + 1) * DH], pa[0:TS, h * TS:(h + 1) * TS],
                       start=True, stop=True)
            i.then_inc(o_full, 1)

            def scores(h):
                z = ps[:, h % 2]
                mm(z[:, 0:2 * P], proj[:, KP + h, 0:P], proj[:, QP + h, 0:2 * P], start=True, stop=True)
                mm(z[:, 2 * P:3 * P], proj[:, KP + h, P:2 * P], proj[:, QP + h, P:2 * P], start=True, stop=True)\
                    .then_inc(z_full, 1)

            for h in range(2):
                scores(h)
            for h in range(HA):
                tail = ps[:, 2 + h % 2]
                pe.wait_ge(z_sp, h + 2)
                mm(tail[:, 0:3 * P], later[:], pspm[:], start=True, stop=True)
                mm(tail[:, P:2 * P], ones[:], pspm[:, 2 * P:3 * P], start=False, stop=True, skip_group_check=True)\
                    .then_inc(tail_full, 1)
                pe.wait_ge(w_ready, h + 2)
                if h >= 2:
                    pe.wait_ge(o_out, h)
                o = ps[:, 4 + h % 2]
                mm(o[:, 0:2 * P], vtok[:, 0, h * DH:(h + 1) * DH], pw[:, 0:2 * P], start=True, stop=True)
                mm(o[:, P:2 * P], vtok[:, 1, h * DH:(h + 1) * DH], pw[:, 2 * P:3 * P], start=False, stop=True,
                   skip_group_check=True).then_inc(o_full, 1)
                if h + 2 < HA:
                    scores(h + 2)

            pe.wait_ge(o_out, 1 + HA)
            pe.wait_ge(ccol_out, 1)

            def page_T(b, p, n):
                pe.wait_ge(kfull[p % 4], 16 * (2 * b + p // 4 + 1))
                if not (isinstance(n, int) and n < 2):
                    pe.wait_ge(kT_act, n - 1)
                    pe.wait_ge(kT_dve, n - 1)
                for h in range(HA):
                    i = tr(ps[:, 2 * (p % 2) + h // 4, (h % 4) * P:(h % 4 + 1) * P], kring[:, p % 4, h, :], P)
                i.then_inc(kT_full, 1)

            def page_scores(b, p, n):
                pe.wait_ge(kT_act, n + 1)
                pe.wait_ge(kT_dve, n + 1)
                if p == 0:
                    pe.wait_ge(qb_ready, b + 1)
                if p % 4 == 0 and not (isinstance(n, int) and n == 0):
                    pe.wait_ge(zrow_out, 2 * b + p // 4)
                for h in range(HA):
                    i = mm(ps[0:HQ, 4, (p % 4) * P:(p % 4 + 1) * P], qmask[:, h * HQ:(h + 1) * HQ], kt[:, p % 2, h, :],
                           start=(h == 0), stop=(h == HA - 1))
                i.then_inc(page_scored, 1)

            def scores_T(b, half):
                for p in range(4):
                    c0 = (4 * half + p) * HQ
                    i = tr(ps[:, 7, c0:c0 + HQ], zrow[:, half, p, :], HQ)
                i.then_inc(z_T, 1)

            def tails(b):
                pe.wait_ge(dn_suffix, 2 * (b + 1))
                flat = lambda a: a.rearrange("p g h t -> p (g h t)")
                mm(ps[:, 7, NPG * HQ:2 * NPG * HQ], later[:], flat(dsp[:]), start=True, stop=True)
                mm(ps[:, 7, NPG * HQ:(2 * NPG - 1) * HQ], ones[:], flat(later_pages[:, 1:]), start=False, stop=True,
                   skip_group_check=True)
                mm(ps[:, 7, NPG * HQ:2 * NPG * HQ].rearrange("p (g h t) -> p g h t", g=NPG, h=HA), ones[0:TS, :],
                   sp_new[:, :, ds(b * LS, LS)].unsqueeze(1).to_broadcast([TS, NPG, HA, LS]),
                   start=False, stop=True, skip_group_check=True).then_inc(dtail_full, 1)

            def page_sum(b, p):
                pe.wait_ge(vfull[p % 4], 16 * (2 * b + p // 4 + 1))
                if p == 0:
                    pe.wait_ge(dn_w, b + 1)
                    if not (isinstance(b, int) and b == 0):
                        pe.wait_ge(do_out, b)
                for h in range(HA):
                    i = mm(ps[0:LS, 5 + h // 4, (h % 4) * DH:(h % 4 + 1) * DH], dw[:, p, h, :], vring[:, p % 4, h, :],
                           start=(p == 0 and h % 4 == 0), stop=(p == NPG - 1 and h % 4 == 3), skip_group_check=True)
                i.then_inc(page_summed, 1)

            def sums_T(b):
                for h in range(HA):
                    i = tr(ps[:, 5, h * LS:(h + 1) * LS], orow[:, h * DH:(h + 1) * DH], LS)
                i.then_inc(o_T, 1)

            def sequence(b):
                n = b * NPG
                first = isinstance(b, int) and b == 0
                page_T(b, 0, n)
                page_T(b, 1, n + 1)
                if not (isinstance(b, int) and b < 2):
                    pe.wait_ge(orow_out, b - 1)
                page_scores(b, 0, n)
                if not (isinstance(b, int) and b < 2):
                    sums_T(b - 2)
                for p in range(2, NPG):
                    page_T(b, p, n + p)
                    if p == 2 and not first:
                        tails(b - 1)
                    page_scores(b, p - 1, n + p - 1)
                    if p == 5:
                        scores_T(b, 0)
                    if not first:
                        for v in {3: [0], 4: [1, 2], 5: [3], 6: [4], 7: [5]}.get(p, []):
                            page_sum(b - 1, v)
                page_scores(b, NPG - 1, n + NPG - 1)
                if not first:
                    page_sum(b - 1, NPG - 2)
                pe.wait_ge(zrow_out, 2 * b + 2)
                if not first:
                    page_sum(b - 1, NPG - 1)
                scores_T(b, 1)

            sequence(0)
            sequence(1)
            with pe.Fori(2, NB) as b:
                sequence(b)
            tails(NB - 1)
            pe.wait_ge(orow_out, NB - 1)
            sums_T(NB - 2)
            for p in range(NPG):
                page_sum(NB - 1, p)
            pe.wait_ge(orow_out, NB)
            sums_T(NB - 1)

            pe.wait_ge(do_out, NB)
            pe.wait_ge(dt_done, 1)
            for t in range(NT + 1):
                w = P if t < NT else TS
                i = tr(ps[0:w, 0, t * HS:(t + 1) * HS], dA_T[:, t * P:t * P + w], HS)
            i.then_inc(dA_full, 1)
            pe.wait_ge(dA_ready, 1)
            for t in range(NT):
                mm(ps[:, 1, t * HS:(t + 1) * HS], incl[:], dA_tok[:, t, :], start=True, stop=True)
                mm(ps[0:HS, 2, t * P:(t + 1) * P], dA_tok[:, t, :], incl[:], start=True, stop=True)
            mm(ps[0:TS, 1, NT * HS:(NT + 1) * HS], incl_s[:], dA_tok[0:TS, NT, :], start=True, stop=True)
            mm(ps[0:HS, 2, SEQ:T], dA_tok[0:TS, NT, :], incl_s[:], start=True, stop=True)
            mm(ps[:, 3, 0:HS], later[:], dA_tok[:, 0, :], start=True, stop=True)
            mm(ps[:, 3, HS:2 * HS], later[:], dA_tok[:, 0, :], start=True, stop=False)
            mm(ps[:, 3, HS:2 * HS], ones[:], dA_tok[:, 1, :], start=False, stop=True)
            mm(ps[:, 3, 2 * HS:3 * HS], later[:], dA_tok[:, 1, :], start=True, stop=True)
            mm(ps[0:TS, 3, 3 * HS:4 * HS], later_s[:], dA_tok[0:TS, NT, :], start=True, stop=True)
            for c in range(SC):
                i = mm(ps[:, 4, c:c + 1], sel[:, c, :], dskip[:], start=True, stop=True)
            i.then_inc(ac_full, 1)
            pe.wait_ge(ac_out, 1)
            pe.wait_ge(ac_exp, 1)
            for c in range(SC):
                if c >= 2:
                    pe.wait_ge(xdt_made, c - 1)
                mm(ps[:, 4 + c % 2, 0:T], sel[:, c, :], dtT[:], start=True, stop=True).then_inc(dtE_full, 1)
                if c >= 2:
                    pe.wait_ge(eaE_made, c - 1)
                mm(ps[:, 6 + c % 2, 0:P + TS], sel[:, c, :], acT[:, P:T], start=True, stop=True).then_inc(acE_full, 1)
            pe.wait_ge(xdt_made, SC)
            for t in range(NT + 1):
                w = P if t < NT else TS
                if t == 2:
                    pe.wait_ge(xdt_out, 1)
                for c in range(SC):
                    i = tr(ps[0:w, 2 * (t % 2) + c // 4, (c % 4) * P:(c % 4 + 1) * P], xdtT[:, c, t * P:t * P + w], P)
                i.then_inc(xdt_full, 1)
            pe.wait_ge(eaE_made, SC)
            for t in range(NT + 1):
                w = P if t < NT else TS
                for g in range(G):
                    i = tr(ps[0:w, 4 + t // 2, (t % 2) * G * NS + g * NS:(t % 2) * G * NS + (g + 1) * NS],
                           xc[:, SC + g, t * P:t * P + w], P)
            i.then_inc(B_full, 1)
            for g in range(G):
                for t in range(NT + 1):
                    w = P if t < NT else TS
                    i = mm(ps[0:w, 6 + g, t * P:t * P + w], xc[:, SC + g, t * P:t * P + w],
                           xc[:, SC + G + g, t * P:t * P + w], start=True, stop=True)
            i.then_inc(cb_full, 1)

            pe.wait_ge(B_out, 1)
            pe.wait_ge(xde_made, 1)
            pe.wait_ge(xdt_out, 3)
            for g in range(G):
                i = mm(ps[:, g, :], B_tok[:, 0, g, :], xde[:, 0, g * GCH * P:(g + 1) * GCH * P], start=True, stop=True)
            i.then_inc(h1_full, 1)

            pe.wait_ge(cbm_made, 1)
            pe.wait_ge(hb_ready, 1)
            pe.wait_ge(h1_out, 1)

            def sums_to_all(h):
                if h >= 2:
                    pe.wait_ge(seg_ready, h - 1)
                mm(ps[:, h % 2, 0:T], hb[:, h, :], acT[:], start=True, stop=True).then_inc(bc_full, 1)

            def y_diag(h):
                c, a = divmod(h, 2)
                pe.wait_ge(sco_ready, h + 1)
                if c >= 2:
                    pe.wait_ge(yd_out, c - 1)
                for t in range(NT + 1):
                    w = P if t < NT else TS
                    i = mm(ps[a * PD:(a + 1) * PD, 2 + c % 2, t * P:t * P + w], xdt_tok[0:w, t, h * PD:(h + 1) * PD],
                           sco[0:w, h % 2, t * P:t * P + w], start=True, stop=True)
                i.then_inc(yd_full, 1)

            sums_to_all(0)
            for h in range(HS):
                if h + 1 < HS:
                    sums_to_all(h + 1)
                y_diag(h)

            for c in range(SC):
                i = mm(ps[:, 4 + c // 4, (c % 4) * P:(c % 4 + 1) * P], h1T[:, c * P:(c + 1) * P],
                       xc[:, SC + G + c // GCH, P:2 * P], start=True, stop=True)
            i.then_inc(yo_full, 1)
            for c in range(SC):
                o = ps[:, 6 + c // 4, (c % 4) * P:(c % 4 + 1) * P]
                mm(o, xde[:, 1, c * P:(c + 1) * P], B_tok[:, 0, c // GCH, :], start=True, stop=False)
                i = mm(o, xde[:, 2, c * P:(c + 1) * P], B_tok[:, 1, c // GCH, :], start=False, stop=True)
            i.then_inc(ssm_full, 1)
            pe.wait_ge(yd_out, SC)
            pe.wait_ge(ssm_out, 1)
            pe.wait_ge(yo_out, 1)
            for b in range(NB):
                pe.wait_ge(h0_full[b % 2], 16 * (b // 2 + 1))
                if b:
                    pe.wait_ge(h0T_out, b)
                for c in range(SC):
                    i = tr(ps[:, c // 4, (c % 4) * P:(c % 4 + 1) * P], h0[:, b % 2, c, :], P)
                i.then_inc(h0T_full, 1)
                pe.wait_ge(bm_ready, b + 1)
                if b:
                    pe.wait_ge(hn_out, b)
                for c in range(SC):
                    i = mm(ps[:, 2 + c // 4, (c % 4) * P:(c % 4 + 1) * P], xde_s[:, c * P:(c + 1) * P],
                           bm_s[:, c // GCH, :], start=True, stop=True)
                i.then_inc(hn_full, 1)
                pe.wait_ge(h0T_out, b + 1)
                for c in range(SC):
                    i = mm(ps[:, 4, (c * NB + b) * LS:(c * NB + b + 1) * LS], h0T[:, c, :],
                           xc[:, SC + G + c // GCH, SEQ + b * LS:SEQ + (b + 1) * LS], start=True, stop=True)
                i.then_inc(ys_full, 1)
            pe.wait_ge(ysq_ready, 1)
            for g in range(G):
                sums(sq1, range(g * GCH, (g + 1) * GCH), 6 + g)

            adaq(4, fold_last=False)
            pe.wait_ge(y_lo, 1)
            pe.wait_ge(ov_lo, 1)
            yx = (lambda k: yhi[:, k, :] if k < SC else ohi[:, k - SC, :]), \
                 (lambda k: ylo[:, k, :] if k < SC else olo[:, k - SC, :])
            pairs(2, 4, *yx)
            fold(4)
            pe.wait_ge(group_free, 2 + ZX_GROUPS + QKV_GROUPS + 4)
            norm_sums(sq2)
            norm_sums(sq2)

            pe.wait_ge(h_lo, 2)

            def up(r, s):
                out0 = r if isinstance(r, int) else 2
                if out0 >= 2:
                    pe.wait_ge(f_add, 4 * r - 5 + s)
                elif r == 1:
                    pe.wait_ge(f_u, s + 1)
                for j in range(RING):
                    pe.wait_ge(lo_ready, 4 * pos.quad + j + 1)
                    unit3(j, 4 * s, lambda q: (h2hi[:, j * QC + q, :], h2lo[:, j * QC + q, :]), j == 0, j == RING - 1)\
                        .then_inc(w_used, 1)
                pos.step(quad=1)

            def down(r, last=False):
                pe.wait_ge(f_lo, r + 1)
                for n in range(4):
                    if n < 2:
                        if last:
                            pe.wait_ge(f_add, 4 * r - 1 + n)
                        else:
                            pe.wait_ge(f_u, 2 * r + 3 + n)
                    else:
                        pe.wait_ge(f_add, 4 * r + n - 1)
                    pe.wait_ge(lo_ready, 4 * pos.quad + n + 1)
                    unit3(n, 4 * (n % 2), lambda q: (ghi[:, q, :], glo[:, q, :]), True, True).then_inc(w_used, 1)
                pos.step(quad=1)

            ROUNDS = FC // MC
            up(0, 0)
            up(0, 1)
            up(1, 0)
            up(1, 1)
            down(0)
            with pe.Fori(2, ROUNDS) as r:
                pos.enter(r, 2, quad=3)
                up(r, 0)
                up(r, 1)
                down(r - 1)
                pos.leave(ROUNDS - 2)
            down(ROUNDS - 1, last=True)

            norm_sums(sq3)
            pe.wait_ge(f_col, 2 * ROUNDS)
            pe.wait_ge(fcomp_ready, 1)
            for n in range(11):
                i = tr(ps[:, 5 + n // 4, (n % 4) * P:(n % 4 + 1) * P], fcomp[:, n, :], P)
            i.then_inc(fc_T, 1)
            for r in range(2):
                i = tr(ps[0:2 * FC, 4, r * P:(r + 1) * P], pcol[:, :, r], P)
            i.then_inc(fc_T, 1)
            pe.wait_ge(fc_o, 2)
            pe.wait_ge(x2_ready, 2)
            for n in range(4 * (NT + 1)):
                t, g = divmod(n, 4)
                w = P if t < NT else TS
                if n >= 8:
                    pe.wait_ge(ys_o, n - 7)
                for m in range(4):
                    i = tr(ps[0:w, n % 8, m * P:(m + 1) * P], xT[:, 4 * g + m, t * P:t * P + w], P)
                i.then_inc(ys_T, 1)

        @block.scalar
        def _(act):
            pos = Place()
            c = Count(act, act_c)
            fn = act.activation

            for r0, src in ((0, c_prompt), (1, c_sample)):
                act.dma_start(crow[r0:r0 + src.shape[0]], src).then_inc(in_c, 16)
            for n, r0, src in ((0, 0, b_ada), (0, MODC, g_pre_mix), (0, MODC + KC, g_post_mix), (1, 0, g_pre_ffn),
                               (1, KC, g_post_ffn), (1, V_CB, conv_b), (1, V_GS, g_ssd_norm), (2, 0, ffn_conv_b)):
                k = src.shape[1] // P
                act.dma_start(vrow[r0:r0 + k, n, :], src[0].rearrange("(c p) -> c p", p=P)).then_inc(in_vec, 16)
            act.dma_start(vrow[V_CW:V_CB, 1, :], conv_w[0].rearrange("k (c p) -> (k c) p", p=P)).then_inc(in_vec, 16)
            act.dma_start(vrow[0:2 * FC, 3:6, :], ffn_conv_w[0].rearrange("k (c p) -> c k p", p=P)).then_inc(in_vec, 16)
            for t in range(NT):
                act.dma_start(xrow[:, t, :], x_prompt[0, t * P:(t + 1) * P]).then_inc(in_x, 16)
            act.dma_start(xrow[0:TS, NT, :], x_sample.rearrange("b t d -> (b t) d")).then_inc(in_x, 16)
            act.dma_start(frow[:].rearrange("p c f -> p (c f)"),
                          state_ffn_conv[0].rearrange("b r (g x) -> (b r g) x", g=8)).then_inc(in_ctx, 16)
            act.dma_start(srow[0:96].rearrange("p c f -> p (c f)"),
                          state_conv[0].rearrange("b r (g x) -> (b r g) x", g=4)).then_inc(in_ctx, 16)
            for dst, src in ((dtb, dt_bias), (nega, a_log), (dskip, d_skip)):
                act.dma_start(dst[:], src.rearrange("o h -> h o")).then_inc(in_misc, 16)
            act.dma_start(sbb[:], sb_bias.to_broadcast([P, HA])).then_inc(in_misc, 16)
            act.dma_start(wdt[:], w_in_v[:, COL_DT:COL_Q].rearrange("(k p) n -> p k n", p=P)).then_inc(in_misc, 16)
            act.dma_start(ptab[:], page_table.rearrange("b n -> (b n)").unsqueeze(0)).then_inc(in_pt, 16)

            act.wait_ge(rows_T, 4)
            fn(cT[:].rearrange("p k s -> p (k s)"), ps[:, 1, 256:256 + KC * NSEQ], ACT.Silu).then_inc(c_ready, 1)
            act.wait_ge(c_ready, 1)
            fn(cs[:, :, 0:NSEQ], cT[:], ACT.Copy).then_inc(cs_hi, 1)
            for n in range(12):
                t, g = divmod(n, 4)
                w = P if t < NT else TS
                act.wait_ge(x_T, n + 1)
                fn(xT[:, 4 * g:4 * g + 4, t * P:t * P + w],
                   ps[:, (6 + n) % 8, 0:4 * w].rearrange("p (m w) -> p m w", m=4), ACT.Copy).then_inc(x_out, 1)
            act.wait_ge(x_out, 12)
            act.sem_inc(group_free, 2)
            norms = [0]

            def square(dst, src):
                fn(dst[:], src[:], ACT.Square).then_inc(sq_ready, 1)

            def root(bank, dst, width):
                norms[0] += 1
                act.wait_ge(sum_ready, norms[0])
                fn(dst, ps[:, bank, 0:T], ACT.Sqrt, scale=1.0 / width, bias=eps[:]).then_inc(root_ready, 1)

            modulated = [0]

            def modulate(f, hi, shift):
                modulated[0] += 1
                act.wait_ge(xr_ready, modulated[0])
                for k in range(KC):
                    i = fn(f[:, k, 0:SEQ], f[:, k, 0:SEQ], ACT.Identity, scale=gainT[:, k, 0:1], bias=modT[:, shift + k, 0:1])
                i.then_inc(hp_ready, 1)
                act.wait_ge(hp_ready, modulated[0])
                act.wait_ge(hs_ready, modulated[0])
                fn(hi[:], f[:], ACT.Copy).then_inc(h_hi, 1)

            def hi(j):
                act.wait_ge(raw_full[j], 16 * (pos.quad + 1))
                if not (isinstance(pos.quad, int) and 4 * pos.quad + j < 2):
                    act.wait_ge(w_used, 4 * pos.quad + j - 1)
                fn(whi[:, j % 2], raw[:, j], ACT.Copy).then_inc(hi_ready, 1)

            def ada():
                for j in range(RING):
                    hi(j)
                pos.step(quad=1)

            square(sq0, xT)
            act.wait_ge(consts, 2)
            root(2, rT[:], DM)
            ada()
            with act.Fori(1, 8) as i:
                pos.enter(i, 1, quad=1)
                ada()
                pos.leave(7)
            modulate(hf, hhi, SH1)
            act.wait_ge(dt_full, 1)
            fn(dtraw[:], ps[0:HS, 7, 0:T], ACT.Copy).then_inc(dt_out, 1)

            def pair(out, chunk):
                for j in range(RING):
                    hi(j)
                pos.step(quad=1)
                for j in range(RING):
                    hi(j)
                    if j == 1:
                        act.wait_ge(w_used, 4 * pos.quad)
                        b = 4 * side[0]
                        fn(out[:, ds(chunk, MC), :], ps[:, b:b + 4, 0:T], ACT.Copy).then_inc(group_free, 1)
                        side[0] ^= 1
                pos.step(quad=1)

            side = [0]
            pair(proj, 0)
            with act.Fori(0, 2) as i:
                pos.enter(i, 0, quad=4)
                pair(proj, i * (2 * MC) + MC)
                pair(proj, i * (2 * MC) + 2 * MC)
                pos.leave(2)
            with act.Fori(0, 3) as i:
                pos.enter(i, 0, quad=4)
                pair(proj, i * (2 * MC) + QP)
                pair(proj, i * (2 * MC) + QP + MC)
                pos.leave(3)

            for t in range(NT + 1):
                w = P if t < NT else TS
                act.wait_ge(tok_full, t + 1)
                if t:
                    act.wait_ge(tok_dma, 16 * t)
                fn(kstage[0:w].rearrange("p (b x) -> p b x", b=2), ps[0:w, 2 * (t % 2):2 * (t % 2) + 2, :], ACT.Copy)\
                    .then_inc(ktok_out, 1)
            act.wait_ge(ccol_T, 1)
            fn(cout[:], ps[0:108, 7, 0:3 * P].rearrange("p (c f) -> p c f", c=3), ACT.Copy).then_inc(ccol_out, 1)

            n_z = [0]

            def soft(x):
                n_z[0] += 1
                act.wait_ge(z_na, n_z[0])
                c.link(fn(x, x, ACT.Exp))
                fn(x, x, ACT.Ln, bias=1.0).then_inc(z_e, 1)

            soft(pa[0:TS, 0:HA * TS])
            act.wait_ge(w_d, 1)
            fn(pa[0:TS, 0:HA * TS], pz[0:TS, 0:HA * TS], ACT.Exp).then_inc(w_e, 1)
            for h in range(HA):
                soft(pa[:])
                act.wait_ge(w_d, h + 2)
                fn(pw[:], pz[:], ACT.Exp).then_inc(w_e, 1)

            def k_half(p, n):
                act.wait_ge(kT_full, n + 1)
                if not (isinstance(n, int) and n < 2):
                    act.wait_ge(page_scored, n - 1)
                fn(kt[:, p % 2, 0:4, :], ps[:, 2 * (p % 2), :].rearrange("p (h x) -> p h x", h=4), ACT.Copy)\
                    .then_inc(kT_act, 1)

            def weights(b):
                act.wait_ge(dn_d, b + 1)
                if not (isinstance(b, int) and b == 0):
                    act.wait_ge(page_summed, b * NPG)
                fn(dw[:], dz[:], ACT.Exp).then_inc(dn_w, 1)

            def rows_of_scores(b, half):
                act.wait_ge(page_scored, NPG * b + 4 * (half + 1))
                fn(zrow[:, half].rearrange("p g k -> p (g k)"), ps[0:HQ, 4, :], ACT.Copy).then_inc(zrow_out, 1)

            def rows_of_sums(b):
                act.wait_ge(page_summed, NPG * (b + 1))
                fn(orow[:].rearrange("p (b x) -> p b x", b=2), ps[0:LS, 5:7, :], ACT.Copy).then_inc(orow_out, 1)

            def sequence(b):
                first = isinstance(b, int) and b == 0
                for p in range(NPG):
                    k_half(p, b * NPG + p)
                    if p == 2 and not first:
                        weights(b - 1)
                    if p == 4:
                        rows_of_scores(b, 0)
                rows_of_scores(b, 1)
                if not first:
                    rows_of_sums(b - 1)
                act.wait_ge(dn_na, b + 1)
                c.link(fn(da[:], da[:], ACT.Exp))
                fn(da[:], da[:], ACT.Ln, bias=1.0).then_inc(dn_e, 1)

            sequence(0)
            sequence(1)
            with act.Fori(2, NB) as b:
                c.enter(b, 2, 1)
                sequence(b)
                c.leave(NB - 2)
            weights(NB - 1)
            rows_of_sums(NB - 1)

            act.wait_ge(do_out, NB)
            fn(ohi[:], oT[:], ACT.Copy).then_inc(ov_hi, 1)
            fn(proj[:, ZP:ZP + SC, :], proj[:, ZP:ZP + SC, :], ACT.Silu).then_inc(z_silu, 1)
            act.wait_ge(conv_done, 1)
            fn(xc[:], xc[:], ACT.Silu).then_inc(silu_done, 1)
            act.wait_ge(in_misc, 16 * 5)
            fn(nega[:], nega[:], ACT.Exp).then_inc(a_ready, 1)
            act.wait_ge(dt_na, 1)
            fn(t2[:], t2[:], ACT.Exp).then_inc(dt_e, 1)
            act.wait_ge(dt_e, 1)
            fn(dtT[:], t2[:], ACT.Ln, bias=1.0).then_inc(dt_ln, 1)
            act.wait_ge(ac_full, 1)
            for t in range(4):
                w = P if t < 3 else TS
                i = fn(dend_tok[0:w, t, :], ps[0:w, 3, t * HS:(t + 1) * HS], ACT.Exp)
            i.then_inc(ac_exp, 1)
            for k in range(SC):
                act.wait_ge(acE_full, k + 1)
                fn(eaE[:, k, :], ps[:, 6 + k % 2, 0:P + TS], ACT.Exp).then_inc(eaE_made, 1)
            act.wait_ge(B_full, 1)
            fn(B_tok[:, 0:2], ps[:, 4, :].rearrange("p (t g n) -> p t g n", t=2, g=G), ACT.Copy)
            fn(B_tok[0:TS, 2], ps[0:TS, 5, 0:G * NS].rearrange("p (g n) -> p g n", g=G), ACT.Copy).then_inc(B_out, 1)
            act.wait_ge(h1_full, 1)
            fn(h1T[:].rearrange("p (g x) -> p g x", g=G), ps[:, 0:2, :], ACT.Copy).then_inc(h1_out, 1)
            for h in range(HS):
                act.wait_ge(seg_ready, h + 1)
                if h >= 2:
                    act.wait_ge(sco_ready, h - 1)
                fn(dec[:, h % 2], seg[:, h % 2], ACT.Exp).then_inc(dec_ready, 1)
            for b in range(NB):
                act.wait_ge(h0T_full, b + 1)
                if b:
                    act.wait_ge(ys_full, b)
                fn(h0T[:].rearrange("p (b c) x -> p b (c x)", b=2), ps[:, 0:2, :], ACT.Copy).then_inc(h0T_out, 1)
            act.wait_ge(y_gated, 1)
            fn(sq1[:], yT[:], ACT.Square).then_inc(ysq_ready, 1)
            for g in range(G):
                root(6 + g, rg[:, g], GCH * P)
            act.wait_ge(y_normed, 1)
            for k in range(SC):
                i = fn(yhi[:, k, :], yT[:, k, :], ACT.Copy, scale=vecT[:, 1, V_GS + k:V_GS + k + 1])
            i.then_inc(y_hi, 1)

            side[0] = 1
            for half in range(2):
                act.wait_ge(hn_dma[half], 16 * (NB // 2))
            ada()
            with act.Fori(0, 2) as i:
                pos.enter(i, 0, quad=4)
                pair(mT, i * (2 * MC))
                pair(mT, i * (2 * MC) + MC)
                pos.leave(2)
            act.wait_ge(group_free, 2 + ZX_GROUPS + QKV_GROUPS + 4)
            square(sq2, mT)
            root(2, rT[:], DM)
            act.wait_ge(x2_ready, 1)
            square(sq2, xT)
            root(2, rT[:], DM)
            modulate(h2f, h2hi, SH2)

            def high_g(r):
                act.wait_ge(f_gt, r + 1)
                if not (isinstance(r, int) and r == 0):
                    act.wait_ge(w_used, split_g[0])
                fn(ghi[:], gt[:], ACT.Copy).then_inc(f_hi, 1)

            split_g = [0]

            def out_of_psum(r, s):
                u = (ug, uv)[s]
                if not (isinstance(r, int) and r == 0):
                    act.wait_ge(f_c, 2 * (r - 1) + s + 1)
                    act.wait_ge(f_col, 2 * (r - 1) + s + 1)
                fn(u[:, :, 2:2 + SEQ], ps[:, 4 * s:4 * s + 4, 0:SEQ], ACT.Copy)
                fn(u[:, :, SEQ + 2:UP].rearrange("p m (b t) -> p m b t", b=NB)[:, :, :, 2:2 + LS],
                   ps[:, 4 * s:4 * s + 4, SEQ:T].rearrange("p m (b t) -> p m b t", b=NB), ACT.Copy).then_inc(f_u, 1)

            def silu(r):
                act.wait_ge(f_c, 2 * r + 1)
                fn(cg[:, :, 0:UP - 2], cg[:, :, 0:UP - 2], ACT.Silu).then_inc(f_s, 1)

            def round_(r, out):
                for s in range(2):
                    hi(0)
                    hi(1)
                    if s == 0 and out:
                        split_g[0] = 4 * pos.quad
                        high_g(r - 1)
                    if s == 1:
                        act.wait_ge(w_used, 4 * pos.quad)
                        out_of_psum(r, 0)
                    hi(2)
                    hi(3)
                    pos.step(quad=1)
                if out:
                    hi(0)
                    hi(1)
                act.wait_ge(w_used, 4 * pos.quad)
                out_of_psum(r, 1)
                silu(r)
                if out:
                    hi(2)
                    hi(3)
                    pos.step(quad=1)

            ROUNDS = FC // MC
            round_(0, False)
            round_(1, True)
            with act.Fori(2, ROUNDS) as r:
                pos.enter(r, 2, quad=3)
                round_(r, True)
                pos.leave(ROUNDS - 2)
            split_g[0] = 4 * pos.quad
            high_g(ROUNDS - 1)
            for j in range(RING):
                hi(j)
            pos.step(quad=1)
            act.wait_ge(f_add, 4 * ROUNDS)
            square(sq3, fT)
            root(2, rT[:], DM)
            act.wait_ge(fc_T, 2)
            fn(fstage[:, 0:8].rearrange("p (b c) f -> p b (c f)", b=2), ps[:, 5:7, :], ACT.Copy)
            fn(fstage[:, 8:11].rearrange("p c f -> p (c f)"), ps[:, 7, 0:3 * P], ACT.Copy).then_inc(fc_o, 1)
            fn(fpstage[:].rearrange("p r f -> p (r f)"), ps[0:2 * FC, 4, 0:2 * P], ACT.Copy).then_inc(fc_o, 1)

        @block.vector
        def _(dve):
            pos = Place()
            c = Count(dve, dve_c)
            tt, ts, stt, cp = dve.tensor_tensor, dve.tensor_scalar, dve.scalar_tensor_tensor, dve.tensor_copy
            MUL, ADD, SUB, MIN, MAX = ALU.mult, ALU.add, ALU.subtract, ALU.min, ALU.max

            dve.wait_ge(consts, 2)
            dve.wait_ge(rows_T, 4)
            for n, k in ((0, P), (1, V_GS + SC)):
                cp(vecT[:, n, 0:k], ps[:, 0, n * P:n * P + k])
            cp(vecT[:, 2:4, 0:2 * FC], ps[:, 0, 2 * P:4 * P].rearrange("p (v k) -> p v k", v=2)[:, :, 0:2 * FC])
            dve.wait_ge(c_ready, 1)
            c.mark(cp(vecT[:, 4:6, 0:2 * FC], ps[:, 1, 0:2 * P].rearrange("p (v k) -> p v k", v=2)[:, :, 0:2 * FC]))
            rows = ctxT[:].rearrange("p (g c) r -> p c r g", c=11)
            for n in range(3):
                k = min(4, 11 - 4 * n)
                cp(rows[:, 4 * n:4 * n + k], ps[:, 2 + n, 0:k * P].rearrange("p (c r g) -> p c r g", c=k, g=8))
            for g in range(4):
                i = cp(xpad[:, 3 * g:3 * g + 3, :, 0:KCONV - 1],
                       ps[:, 5, 0:288].rearrange("p (c b k g) -> p g c b k", c=3, b=NB, g=4)[:, g])
            i.then_inc(rows_out, 1)
            dve.wait_ge(in_misc, 16 * 5)
            c.mark(cp(zbias[:], sbb[:].unsqueeze(1).unsqueeze(3).to_broadcast([P, NPG, HA, LS])))

            dve.wait_ge(cs_hi, 1)
            tt(cs[:, :, NSEQ:], cT[:], cs[:, :, 0:NSEQ].bitcast(F32), SUB).then_inc(cs_ready, 1)

            def lo(j):
                dve.wait_ge(hi_ready, 4 * pos.quad + j + 1)
                tt(wlo[:, j % 2], raw[:, j], whi[:, j % 2].bitcast(F32), SUB).then_inc(lo_ready, 1)

            def rows_of(bank):
                dve.wait_ge(w_used, 4 * pos.quad)
                cp(arow[:], ps[0:2 * NSEQ, bank + 3, :]).then_inc(ada_row, 1)

            def mod_of(bank):
                dve.wait_ge(fold_full, pos.ada)
                n = (pos.ada - 1) * MC
                tt(modT[:, ds(n, MC), :], ps[:, bank + 2, 0:MC * NSEQ].rearrange("p (m s) -> p m s", m=MC),
                   vecT[:, 0, ds(n, MC)].unsqueeze(2).to_broadcast([P, MC, NSEQ]), ADD).then_inc(mod_ready, 1)

            c.settle()
            norms = [0]

            def normed(dst, src, r, chunks):
                norms[0] += 1
                dve.wait_ge(root_ready, norms[0])
                c.link(dve.reciprocal(r, r))
                return tt(dst, src, r.unsqueeze(1).to_broadcast([P, chunks, T]), MUL)

            def gain(scale, g, plus):
                vec = vecT[:, g[0], g[1]:g[1] + KC].unsqueeze(2).to_broadcast([P, KC, NSEQ])
                return stt(gainT[:], modT[:, scale:scale + KC, :], plus, vec, ADD, MUL)

            def per_seq(m):
                return m[:, :, 1:NSEQ].unsqueeze(3).to_broadcast([P, KC, NB, LS])

            def quad(after_0=None, after_1=None):
                for j in range(RING):
                    lo(j)
                    if j == 0 and after_0:
                        after_0()
                    if j == 1 and after_1:
                        after_1()
                pos.step(quad=1)

            quad()
            pos.step(ada=1)
            with dve.Fori(1, 8) as i:
                pos.enter(i, 1, quad=1, ada=1)
                quad(lambda: rows_of(4), lambda: mod_of(4))
                pos.step(ada=1)
                pos.leave(7)
            rows_of(4)
            mod_of(4)
            dve.wait_ge(mod_ready, 8)

            def prepare(f, src, scale, shift, g, n):
                c.mark(gain(scale, g, 1.0))
                normed(f[:], src[:], rT[:], KC).then_inc(xr_ready, 1)
                dve.wait_ge(xr_ready, n)
                c.link(tt(smp(f), smp(f), per_seq(gainT), MUL))
                tt(smp(f), smp(f), per_seq(modT[:, shift:shift + KC, :]), ADD).then_inc(hs_ready, 1)

            def low(lo_, f, hi_, n):
                dve.wait_ge(h_hi, n)
                tt(lo_[:], f[:], hi_[:].bitcast(F32), SUB).then_inc(h_lo, 1)

            prepare(hf, xT, SC1, SH1, V_PRE_MIX, 1)
            low(hlo, hf, hhi, 1)

            def pair(bank0):
                quad(lambda: rows_of(bank0))
                quad(None, lambda: mod_of(4 - bank0))
                pos.step(ada=1)

            def pairs(turns, bank0):
                with dve.Fori(0, turns) as i:
                    pos.enter(i, 0, quad=4, ada=2)
                    pair(bank0)
                    pair(4 - bank0)
                    pos.leave(turns)

            quad()
            quad()
            pos.step(ada=1)
            pairs(2, 4)
            pairs(3, 4)
            rows_of(4)
            mod_of(4)

            dve.wait_ge(group_free, 2 + ZX_GROUPS + QKV_GROUPS)
            for g in range(4):
                chunks = slice(XP + 3 * g, XP + 3 * g + 3)
                cp(ccol[:, :, 0:3, g], proj[:, chunks, SEQ - 3:SEQ])
                i = cp(ccol[:, :, 3:27, g].rearrange("p c (b k) -> p c b k", b=NB), smp(proj)[:, chunks, :, LS - 3:LS])
            i.then_inc(ccol_ready, 1)
            c.mark(cp(xpad[:, :, :, KCONV - 1:], smp(proj)[:, XP:XP + XC]))
            for t in range(NT + 1):
                w = P if t < NT else TS
                n = 3 + t
                dve.wait_ge(tok_full, n + 1)
                cp(vtok[0:w, t, :].rearrange("p (b x) -> p b x", b=2), ps[0:w, 2 * (n % 2):2 * (n % 2) + 2, :])\
                    .then_inc(vtok_out, 1)

            nh = [0]

            def softplus(z, a, sp, spm, mask):
                nh[0] += 1
                dve.wait_ge(z_e, nh[0])
                c.link(stt(sp, z, 0.0, a, MAX, ADD))
                tt(spm, sp, mask, MUL).then_inc(z_sp, 1)
                c.link(tt(z, z, sp, SUB))
                dve.wait_ge(tail_full, nh[0])

            HT = HA * TS
            dve.wait_ge(z_full, 1)
            c.link(ts(pz[0:TS, 0:HT], ps[0:TS, 4, 0:HT], SCALE, None, MUL))
            h_t = lambda a: a[0:TS, 0:HT].rearrange("p (h t) -> p h t", h=HA)
            c.link(tt(h_t(pz), h_t(pz), sbb[0:TS].unsqueeze(2).to_broadcast([TS, HA, TS]), ADD))
            stt(pa[0:TS, 0:HT], pz[0:TS, 0:HT], -1.0, pz[0:TS, 0:HT], MUL, MIN).then_inc(z_na, 1)
            mask_s = before_s[:].unsqueeze(1).to_broadcast([TS, HA, TS])
            nh[0] += 1
            dve.wait_ge(z_e, 1)
            c.link(stt(psp[0:TS, 0:HT], pz[0:TS, 0:HT], 0.0, pa[0:TS, 0:HT], MAX, ADD))
            tt(sp_new[:], h_t(psp), mask_s, MUL).then_inc(z_sp, 1)
            c.link(tt(pz[0:TS, 0:HT], pz[0:TS, 0:HT], psp[0:TS, 0:HT], SUB))
            dve.wait_ge(tail_full, 1)
            tt(pz[0:TS, 0:HT], pz[0:TS, 0:HT], ps[0:TS, 5, 0:HT], SUB).then_inc(w_d, 1)
            dve.wait_ge(w_e, 1)
            tt(h_t(pa), h_t(pa), mask_s, MUL).then_inc(w_ready, 1)
            dve.wait_ge(o_full, 1)
            cp(o_new[:].rearrange("p h t -> p (h t)"), ps[:, 6, 0:HT]).then_inc(o_out, 1)
            for h in range(HA):
                dve.wait_ge(z_full, h + 2)
                c.link(ts(pz[:], ps[:, h % 2, 0:3 * P], SCALE, sbb[:, h:h + 1], MUL, ADD))
                stt(pa[:], pz[:], -1.0, pz[:], MUL, MIN).then_inc(z_na, 1)
                softplus(pz[:], pa[:], psp[:], pspm[:], cmask[:])
                tt(pz[:], pz[:], ps[:, 2 + h % 2, 0:3 * P], SUB).then_inc(w_d, 1)
                dve.wait_ge(w_e, h + 2)
                tt(pw[:], pw[:], cmask[:], MUL).then_inc(w_ready, 1)
                dve.wait_ge(o_full, h + 2)
                cp(oT[:, h, 0:SEQ], ps[:, 4 + h % 2, 0:SEQ]).then_inc(o_out, 1)

            def k_half(p, n):
                dve.wait_ge(kT_full, n + 1)
                if not (isinstance(n, int) and n < 2):
                    dve.wait_ge(page_scored, n - 1)
                cp(kt[:, p % 2, 4:8, :], ps[:, 2 * (p % 2) + 1, :].rearrange("p (h x) -> p h x", h=4)).then_inc(kT_dve, 1)

            flat = lambda a: a[:].rearrange("p g h t -> p (g h t)")

            def log_weights(b):
                dve.wait_ge(dtail_full, b + 1)
                tt(flat(dz), flat(dz), ps[:, 7, NPG * HQ:2 * NPG * HQ], SUB).then_inc(dn_d, 1)

            def summed(b):
                dve.wait_ge(o_T, b + 1)
                tt(oT[:, :, ds(b * LS + SEQ, LS)], ps[:, 5, 0:HQ].rearrange("p (h t) -> p h t", h=HA),
                   o_new[:, :, ds(b * LS, LS)], ADD).then_inc(do_out, 1)

            def sequence(b):
                first = isinstance(b, int) and b == 0
                for p in range(NPG):
                    k_half(p, b * NPG + p)
                    if p == 1 and not (isinstance(b, int) and b < 2):
                        summed(b - 2)
                    if p == 2 and not first:
                        log_weights(b - 1)
                if not first:
                    dve.wait_ge(dn_w, b)
                dve.wait_ge(z_T, 2 * (b + 1))
                c.link(stt(flat(dz), ps[:, 7, 0:NPG * HQ], SCALE, flat(zbias), MUL, ADD))
                stt(flat(da), flat(dz), -1.0, flat(dz), MUL, MIN).then_inc(dn_na, 1)
                dve.wait_ge(dn_e, b + 1)
                stt(flat(dsp), flat(dz), 0.0, flat(da), MAX, ADD).then_inc(dn_sp, 1)
                dve.wait_ge(dn_sp, b + 1)
                for d, src, dst in ((1, dsp, later_pages), (2, later_pages, da)):
                    c.mark(tt(dst[:, 0:NPG - d], src[:, 0:NPG - d], src[:, d:], ADD))
                    c.link(cp(dst[:, NPG - d:], src[:, NPG - d:]))
                tt(later_pages[:, 0:4], da[:, 0:4], da[:, 4:], ADD).then_inc(dn_suffix, 1)
                cp(later_pages[:, 4:], da[:, 4:]).then_inc(dn_suffix, 1)
                c.link(tt(flat(dz), flat(dz), flat(dsp), SUB))

            dve.wait_ge(ccol_dma, 32)
            sequence(0)
            sequence(1)
            with dve.Fori(2, NB) as b:
                c.enter(b, 2, 6)
                sequence(b)
                c.leave(NB - 2)
            log_weights(NB - 1)
            summed(NB - 2)
            summed(NB - 1)
            dve.wait_ge(ov_hi, 1)
            tt(olo[:], oT[:], ohi[:].bitcast(F32), SUB).then_inc(ov_lo, 1)

            dve.wait_ge(tok_dma, 16 * 6)
            cw = lambda k, x: vecT[:, 1, V_CW + k * XC + x:V_CW + k * XC + x + 1]
            for x in range(XC):
                i = ts(xc[:, x, 0:SEQ], proj[:, XP + x, 0:SEQ], cw(KCONV - 1, x), vecT[:, 1, V_CB + x:V_CB + x + 1], MUL, ADD)
            c.link(i)
            for d in range(1, KCONV):
                for x in range(XC):
                    i = stt(xc[:, x, d:SEQ], proj[:, XP + x, 0:SEQ - d], cw(KCONV - 1 - d, x), xc[:, x, d:SEQ], MUL, ADD)
                c.link(i)
            taps = [vecT[:, 1, v:v + XC].unsqueeze(2).unsqueeze(3).to_broadcast([P, XC, NB, LS])
                    for v in [V_CW + k * XC for k in range(KCONV)] + [V_CB]]
            c.link(tt(smp(xc), xpad[:, :, :, 0:LS], taps[0], MUL))
            c.link(tt(smp(xc), smp(xc), taps[KCONV], ADD))
            tmp = ctmp[:].rearrange("p n (b t) -> p n b t", b=NB)
            for k in range(1, KCONV):
                c.link(tt(tmp, xpad[:, :, :, k:k + LS], taps[k], MUL))
                i = tt(smp(xc), smp(xc), tmp, ADD)
                if k < KCONV - 1:
                    c.link(i)
            i.then_inc(conv_done, 1)

            c.link(ts(t1[:], dtraw[:], dtb[:], None, ADD))
            stt(t2[:], t1[:], -1.0, t1[:], MUL, MIN).then_inc(dt_na, 1)
            dve.wait_ge(a_ready, 1)
            c.link(ts(nega[:], nega[:], -1.0, None, MUL))
            dve.wait_ge(dt_ln, 1)
            c.link(ts(acT[:], t2[:], 1.0, None, ADD))
            c.link(ts(acT[:], acT[:], 1.0, None, SUB))
            c.link(ts(dA_T[:], acT[:], 0.0, None, ALU.is_equal))
            c.mark(tt(acT[:], acT[:], dA_T[:], ADD))
            c.link(tt(dtT[:], dtT[:], dA_T[:], ADD))
            c.mark(dve.reciprocal(acT[:], acT[:]))
            c.link(tt(dtT[:], dtT[:], t2[:], MUL))
            c.link(tt(dtT[:], dtT[:], acT[:], MUL))
            c.link(stt(dtT[:], t1[:], 0.0, dtT[:], MAX, ADD))
            ts(dA_T[:], dtT[:], nega[:], None, MUL).then_inc(dt_done, 1)
            dve.wait_ge(dA_full, 1)
            cp(dA_tok[:, 0:NT, :].rearrange("p t h -> p (t h)"), ps[:, 0, 0:NT * HS])
            cp(dA_tok[0:TS, NT, :], ps[0:TS, 0, NT * HS:(NT + 1) * HS]).then_inc(dA_ready, 1)
            dve.wait_ge(ac_full, 1)
            cp(ac_tok[:, 0:NT, :].rearrange("p t h -> p (t h)"), ps[:, 1, 0:NT * HS])
            cp(ac_tok[0:TS, NT, :], ps[0:TS, 1, NT * HS:(NT + 1) * HS])
            cp(acT[:], ps[0:HS, 2, 0:T])
            cp(dskE[:], ps[:, 4, 0:SC]).then_inc(ac_out, 1)
            dve.wait_ge(silu_done, 1)
            for k in range(SC):
                dve.wait_ge(dtE_full, k + 1)
                tt(xdtT[:, k, :], xc[:, k, :], ps[:, 4 + k % 2, 0:T], MUL).then_inc(xdt_made, 1)
            for t in range(NT + 1):
                w = P if t < NT else TS
                dve.wait_ge(xdt_full, t + 1)
                cp(xdt_tok[0:w, t, :].rearrange("p (b x) -> p b x", b=2), ps[0:w, 2 * (t % 2):2 * (t % 2) + 2, :])\
                    .then_inc(xdt_out, 1)
            dve.wait_ge(hb_ready, 1)
            dve.wait_ge(cb_full, 1)
            for g in range(G):
                tt(cbm[:, g, 0:SEQ].rearrange("p (t l) -> p t l", t=NT), ps[:, 6 + g, 0:SEQ].rearrange("p (t l) -> p t l", t=NT),
                   incl[:].unsqueeze(1).to_broadcast([P, NT, P]), MUL)
                i = tt(cbm[0:TS, g, SEQ:T], ps[0:TS, 6 + g, SEQ:T], incl_s[:], MUL)
            i.then_inc(cbm_made, 1)
            dve.wait_ge(ac_exp, 1)
            dve.wait_ge(xdt_out, 3)
            heads = lambda a: a.rearrange("p (h d) -> p h d", d=PD)
            for n, t in ((0, 0), (1, 0), (2, 1)):
                tt(heads(xde[:, n]), heads(xdt_tok[:, t]), dend_tok[:, n, :].unsqueeze(2).to_broadcast([P, HS, PD]), MUL)
            tt(heads(xde_s[:]), heads(xdt_tok[0:TS, NT]), dend_tok[0:TS, 3, :].unsqueeze(2).to_broadcast([TS, HS, PD]), MUL)\
                .then_inc(xde_made, 1)

            def decays(h):
                dve.wait_ge(bc_full, h + 1)
                for t in range(NT + 1):
                    w = P if t < NT else TS
                    i = ts(seg[:, h % 2, t * P:t * P + w], ps[:, h % 2, t * P:t * P + w], ac_tok[:, t, h:h + 1], 0.0, SUB, MIN)
                i.then_inc(seg_ready, 1)

            def weigh(h):
                dve.wait_ge(dec_ready, h + 1)
                if h >= 2:
                    dve.wait_ge(yd_full, h - 1)
                tt(sco[:, h % 2], dec[:, h % 2], cbm[:, h // (HS // G)], MUL).then_inc(sco_ready, 1)

            def diag_out(k):
                dve.wait_ge(yd_full, 2 * k + 2)
                stt(yT[:, k, :], xc[:, k, :], dskE[:, k:k + 1], ps[:, 2 + k % 2, 0:T], MUL, ADD).then_inc(yd_out, 1)

            dve.wait_ge(cbm_made, 1)
            decays(0)
            for h in range(HS):
                if h + 1 < HS:
                    decays(h + 1)
                weigh(h)
                if h % 2 and h > 1:
                    diag_out(h // 2 - 1)
            diag_out(SC - 1)
            dve.wait_ge(yd_out, SC)
            dve.wait_ge(yo_full, 1)
            dve.wait_ge(eaE_made, SC)
            c.link(tt(ytmp[:], eaE[:, :, 0:P], ps[:, 4:6, :].rearrange("p b (c x) -> p (b c) x", c=4), MUL))
            tt(yT[:, :, P:2 * P], yT[:, :, P:2 * P], ytmp[:], ADD).then_inc(yo_out, 1)
            dve.wait_ge(ssm_full, 1)
            cp(hnew[:, 1].rearrange("p (b c) n -> p b (c n)", b=2), ps[:, 6:8, :]).then_inc(ssm_out, 1)
            for b in range(NB):
                if b:
                    dve.wait_ge(hn_full, b)
                ts(bm_s[:].rearrange("p g n -> p (g n)"), B_tok[0:TS, NT].rearrange("p g n -> p (g n)"),
                   seq_of[:, b:b + 1], None, MUL).then_inc(bm_ready, 1)
                dve.wait_ge(hn_full, b + 1)
                if b == 1:
                    dve.wait_ge(ssm_dma, 16)
                if b >= 2:
                    dve.wait_ge(hn_dma[b % 2], 16 * (b // 2))
                for k in range(SC):
                    last_token = P + b * LS + LS - 1
                    i = stt(hnew[:, b % 2, k, :], h0[:, b % 2, k, :], eaE[:, k, last_token:last_token + 1],
                            ps[:, 2 + k // 4, (k % 4) * P:(k % 4 + 1) * P], MUL, ADD)
                i.then_inc(hn_out, 1)
            dve.wait_ge(ys_full, NB)
            c.link(tt(yoff_s[:], eaE[:, :, P:P + TS], ps[:, 4, 0:SC * TS].rearrange("p (c x) -> p c x", c=SC), MUL))
            c.link(tt(yT[:, :, SEQ:T], yT[:, :, SEQ:T], yoff_s[:], ADD))
            dve.wait_ge(z_silu, 1)
            tt(yT[:], yT[:], proj[:, ZP:ZP + SC, :], MUL).then_inc(y_gated, 1)
            dve.wait_ge(y_gated, 1)
            for g in range(G):
                i = normed(yT[:, g * GCH:(g + 1) * GCH], yT[:, g * GCH:(g + 1) * GCH], rg[:, g], GCH)
            i.then_inc(y_normed, 1)
            dve.wait_ge(y_normed, 1)
            dve.wait_ge(y_hi, 1)
            for k in range(SC):
                i = stt(ylo[:, k, :], yT[:, k, :], vecT[:, 1, V_GS + k:V_GS + k + 1], yhi[:, k, :].bitcast(F32), MUL, SUB)
            i.then_inc(y_lo, 1)

            quad()
            pos.step(ada=1)
            pairs(2, 4)
            rows_of(4)
            mod_of(4)
            dve.wait_ge(mod_ready, 24)

            def add_branch(m, gate, g):
                c.mark(normed(m[:], m[:], rT[:], KC))
                c.link(gain(gate, g, 0.0))
                c.link(tt(smp(m), smp(m), per_seq(gainT), MUL))
                for k in range(KC):
                    stt(xT[:, k, 0:SEQ], m[:, k, 0:SEQ], gainT[:, k, 0:1], xT[:, k, 0:SEQ], MUL, ADD)
                tt(smp(xT), smp(xT), smp(m), ADD).then_inc(x2_ready, 1)

            add_branch(mT, G1, V_POST_MIX)
            dve.wait_ge(x2_ready, 1)
            prepare(h2f, xT, SC2, SH2, V_PRE_FFN, 2)
            low(h2lo, h2f, h2hi, 2)

            dve.wait_ge(g2, 1)

            def taps_of(r):
                cols = vecT[:, 2:6, 0:2 * FC].rearrange("p v (s k) -> p v s k", s=2)[:, :, :, ds(r * MC, MC)]
                c.link(cp(fw[:], cols))

            def conv(r, s):
                u, o = ((ug, cg), (uv, cv))[s]
                W = UP - 2
                dve.wait_ge(f_u, 2 * r + s + 1)
                dve.wait_ge(f_ctx, 2 * r + s + 1)
                for k in range(MC):
                    i = ts(o[:, k, 0:W], u[:, k, 2:UP], fw[:, 3, s, k:k + 1], fw[:, 0, s, k:k + 1], MUL, ADD)
                c.link(i)
                for k in range(MC):
                    i = stt(o[:, k, 0:W], u[:, k, 1:1 + W], fw[:, 2, s, k:k + 1], o[:, k, 0:W], MUL, ADD)
                c.link(i)
                for k in range(MC):
                    i = stt(o[:, k, 0:W], u[:, k, 0:W], fw[:, 1, s, k:k + 1], o[:, k, 0:W], MUL, ADD)
                i.then_inc(f_c, 1)

            def product(r):
                dve.wait_ge(f_s, r + 1)
                dve.wait_ge(f_c, 2 * r + 2)
                if not (isinstance(r, int) and r == 0):
                    dve.wait_ge(f_lo, r)
                tt(gt[:, :, 0:SEQ], cg[:, :, 0:SEQ], cv[:, :, 0:SEQ], MUL)
                tt(smp(gt), own(cg), own(cv), MUL).then_inc(f_gt, 1)

            def own(a):
                return a[:, :, SEQ + 2:UP].rearrange("p m (b t) -> p m b t", b=NB)[:, :, :, 0:LS]

            def low_g(r):
                dve.wait_ge(f_hi, r + 1)
                tt(glo[:], gt[:], ghi[:].bitcast(F32), SUB).then_inc(f_lo, 1)

            def add(n, base):
                dve.wait_ge(w_used, base + n + 1)
                b = 4 * (n % 2)
                tt(fT[:, n * MC:(n + 1) * MC, :], fT[:, n * MC:(n + 1) * MC, :], ps[:, b:b + 4, 0:T], ADD).then_inc(f_add, 1)

            def round_(r, out, added):
                taps_of(r)
                lo(0)
                if added:
                    add(3, 4 * pos.quad - 4)
                lo(1)
                if out:
                    low_g(r - 1)
                lo(2)
                lo(3)
                pos.step(quad=1)
                lo(0)
                lo(1)
                conv(r, 0)
                lo(2)
                lo(3)
                pos.step(quad=1)
                if out:
                    lo(0)
                    lo(1)
                conv(r, 1)
                if out:
                    add(0, 4 * pos.quad)
                    lo(2)
                product(r)
                if out:
                    add(1, 4 * pos.quad)
                    lo(3)
                    add(2, 4 * pos.quad)
                    pos.step(quad=1)

            ROUNDS = FC // MC
            round_(0, False, False)
            round_(1, True, False)
            with dve.Fori(2, ROUNDS) as r:
                pos.enter(r, 2, quad=3)
                c.enter(r, 2, 5)
                round_(r, True, True)
                c.leave(ROUNDS - 2)
                pos.leave(ROUNDS - 2)
            add(3, 4 * pos.quad - 4)
            low_g(ROUNDS - 1)
            for n in range(4):
                lo(n)
                if n >= 1:
                    add(n - 1, 4 * pos.quad)
            add(3, 4 * pos.quad)
            dve.wait_ge(f_add, 4 * ROUNDS)
            add_branch(fT, G2, V_POST_FFN)
            for n in range(4 * (NT + 1)):
                t, g = divmod(n, 4)
                w = P if t < NT else TS
                dve.wait_ge(ys_T, n + 1)
                cp(ystage[0:w, t, g * GC:(g + 1) * GC], ps[0:w, n % 8, :]).then_inc(ys_o, 1)


_INS = ['x_prompt', 'x_sample', 'c_prompt', 'c_sample', 'cache_k', 'cache_v', 'page_table', 'state_ssm', 'state_conv',
        'state_ffn_conv', 'w_ada', 'b_ada', 'g_pre_mix', 'g_post_mix', 'g_pre_ffn', 'g_post_ffn', 'w_in', 'conv_w',
        'conv_b', 'dt_bias', 'a_log', 'd_skip', 'g_ssd_norm', 'sb_bias', 'w_out', 'w_ffn_in', 'ffn_conv_w',
        'ffn_conv_b', 'w_ffn_out']
_OUTS = [(1, 256, 2048), (8, 4, 2048), (1, 1, 256, 8, 128), (1, 1, 256, 8, 128), (1, 1, 16, 64, 128), (1, 1, 3, 1536),
         (1, 1, 2, 11264), (1, 8, 4, 8, 128), (1, 8, 4, 8, 128), (1, 8, 16, 64, 128), (1, 8, 3, 1536), (1, 8, 2, 11264)]


def kernel(**inputs):
    import numpy as _np
    import concourse.bacc as _bacc
    from concourse import mybir as _mybir
    from concourse.bass_utils import run_bass_kernel_spmd as _run

    nc = _bacc.Bacc("TRN2", target_bir_lowering=False, num_devices=1)
    arrays, args = {}, []
    for name in _INS:
        a = _np.ascontiguousarray(inputs[name])
        arrays[f"in_{name}_dram"] = a
        args.append(nc.dram_tensor(f"in_{name}_dram", a.shape, _mybir.dt.from_np(a.dtype), kind="ExternalInput").ap())
    for i, shape in enumerate(_OUTS):
        args.append(nc.dram_tensor(f"out_{i}_dram", shape, _mybir.dt.float32, kind="ExternalOutput").ap())
    hybrid_step(nc, *args)
    r = _run(nc, [arrays], core_ids=[0])
    return tuple(r.results[0][f"out_{i}_dram"] for i in range(len(_OUTS)))
```
